# Optimizing a Trainium2 kernel written in Bass

```python
import jax, jax.numpy as jnp
from jax import lax
import numpy as np

D_MODEL = 2048
BATCH = 1
SEQ = 512
DEPTH = 1

ATTN_WIDTH = D_MODEL // 2
ATTN_HEAD_DIM = 128
ATTN_HEADS = ATTN_WIDTH // ATTN_HEAD_DIM
DILATED_PATTERNS = ((128, 1), (512, 4), (2048, 16))
ROPE_THETA = 500000.0
ROPE_DIM = ATTN_HEAD_DIM // 4

GLA_VALUE_WIDTH = D_MODEL - ATTN_WIDTH
GLA_KEY_WIDTH = GLA_VALUE_WIDTH // 2
GLA_HEADS = 4
GLA_DK = GLA_KEY_WIDTH // GLA_HEADS
GLA_DV = GLA_VALUE_WIDTH // GLA_HEADS
GLA_GATE_RANK = 16
GLA_GATE_NORMALIZER = 16.0
GLA_CHUNK = 64

IN_SPLITS = (ATTN_WIDTH, ATTN_WIDTH, ATTN_WIDTH,
             GLA_KEY_WIDTH, GLA_KEY_WIDTH, GLA_VALUE_WIDTH, GLA_VALUE_WIDTH,
             GLA_GATE_RANK, GLA_GATE_RANK)
IN_WIDTH = sum(IN_SPLITS)

D_FF = 5632
CONV_WIDTH = 3
EPS = 1e-6

kernel_name = "hymba_gla_dilated_attn_convglu_encoder"

def rmsnorm(x, g):
    xf = x.astype(jnp.float32)
    y = xf * lax.rsqrt(jnp.mean(xf * xf, axis=-1, keepdims=True) + EPS)
    return (y * g.astype(jnp.float32)).astype(x.dtype)

def apply_partial_rope(t):
    S = t.shape[1]
    pos = jnp.arange(S, dtype=jnp.float32)
    inv_freq = ROPE_THETA ** (-jnp.arange(0, ROPE_DIM, 2, dtype=jnp.float32) / ROPE_DIM)
    ang = pos[:, None] * inv_freq[None, :]
    cos = jnp.cos(ang)[None, :, None, :]
    sin = jnp.sin(ang)[None, :, None, :]
    tr = t[..., :ROPE_DIM].astype(jnp.float32)
    x1, x2 = tr[..., :ROPE_DIM // 2], tr[..., ROPE_DIM // 2:]
    rot = jnp.concatenate([x1 * cos - x2 * sin, x2 * cos + x1 * sin], axis=-1)
    return jnp.concatenate([rot.astype(t.dtype), t[..., ROPE_DIM:]], axis=-1)

def to_residues(t, d):
    B, S = t.shape[:2]
    rest = t.shape[2:]
    t = t.reshape((B, S // d, d) + rest)
    return jnp.swapaxes(t, 1, 2).reshape((B * d, S // d) + rest)

def from_residues(t, d, B):
    N, L = t.shape[:2]
    rest = t.shape[2:]
    t = t.reshape((B, d, L) + rest)
    return jnp.swapaxes(t, 1, 2).reshape((B, L * d) + rest)

def banded_attention(q, k, v, n_side):
    N, L, H, Dh = q.shape
    blk = n_side
    nb = -(-L // blk)
    Lp = nb * blk
    pad = Lp - L
    qb = jnp.pad(q, ((0, 0), (0, pad), (0, 0), (0, 0))).reshape(N, nb, blk, H, Dh)
    kp = jnp.pad(k, ((0, 0), (blk, pad + blk), (0, 0), (0, 0)))
    vp = jnp.pad(v, ((0, 0), (blk, pad + blk), (0, 0), (0, 0)))

    def key_blocks(t):
        return jnp.concatenate(
            [t[:, i * blk:i * blk + Lp].reshape(N, nb, blk, H, Dh) for i in range(3)], axis=2)

    kb, vb = key_blocks(kp), key_blocks(vp)
    s = jnp.einsum('nbqhd,nbkhd->nbhqk', qb, kb).astype(jnp.float32) * (Dh ** -0.5)
    qpos = jnp.arange(nb)[:, None] * blk + jnp.arange(blk)[None, :]
    kpos = jnp.arange(nb)[:, None] * blk - blk + jnp.arange(3 * blk)[None, :]
    qp_, kp_ = qpos[:, :, None], kpos[:, None, :]
    mask = (jnp.abs(kp_ - qp_) <= n_side) & (kp_ >= 0) & ((kp_ < L) | (kp_ == qp_))
    s = jnp.where(mask[None, :, None], s, -jnp.inf)
    m = jnp.max(s, axis=-1, keepdims=True)
    p = jnp.exp(s - m)
    den = jnp.sum(p, axis=-1, keepdims=True)
    lse = (m + jnp.log(den))[..., 0]
    p = p / den
    o = jnp.einsum('nbhqk,nbkhd->nbqhd', p.astype(vb.dtype), vb).reshape(N, Lp, H, Dh)[:, :L]
    lse = jnp.swapaxes(lse, 2, 3).reshape(N, Lp, H)[:, :L]
    return o, lse

def dilated_attention(q, k, v):
    B = q.shape[0]
    outs, lses = [], []
    for window, d in DILATED_PATTERNS:
        n_side = (window // 2) // d
        o, lse = banded_attention(to_residues(q, d), to_residues(k, d), to_residues(v, d), n_side)
        outs.append(from_residues(o, d, B).astype(jnp.float32))
        lses.append(from_residues(lse, d, B))
    w = jax.nn.softmax(jnp.stack(lses), axis=0)
    o = jnp.einsum('pbsh,pbshd->bshd', w, jnp.stack(outs))
    return o.astype(q.dtype)

def gla_chunked(q, k, v, g):
    B, S, H, K = q.shape
    V = v.shape[-1]
    C = GLA_CHUNK
    n = S // C
    q, k, v, g = (t.reshape(B, n, C, H, t.shape[-1]) for t in (q, k, v, g))
    b = jnp.cumsum(g, axis=2)
    b_ref = b[:, :, C // 2 - 1:C // 2]
    b_last = b[:, :, -1]
    a = jnp.einsum('bnihk,bnjhk->bnhij', q * jnp.exp(b - b_ref), k * jnp.exp(b_ref - b))
    a = jnp.where(jnp.tril(jnp.ones((C, C), dtype=bool)), a, 0.0)
    o_intra = jnp.einsum('bnhij,bnjhv->bnihv', a, v)
    q_in = q * jnp.exp(b)
    k_st = k * jnp.exp(b_last[:, :, None] - b)
    dec = jnp.exp(b_last)

    def step(state, xs):
        qc, kc, vc, dc = xs
        o = jnp.einsum('bihk,bhkv->bihv', qc, state)
        state = dc[..., None] * state + jnp.einsum('bjhk,bjhv->bhkv', kc, vc)
        return state, o

    xs = tuple(jnp.moveaxis(t, 1, 0) for t in (q_in, k_st, v, dec))
    _, o_inter = lax.scan(step, jnp.zeros((B, H, K, V), jnp.float32), xs)
    o = o_intra + jnp.moveaxis(o_inter, 0, 1)
    return o.reshape(B, S, H, V)

def hybrid_mixer(h, w_in, gf_up, gf_b, gb_up, gb_b, gla_norm_g, attn_norm_g, w_out):
    B, S, _ = h.shape
    f32 = jnp.float32
    proj = h @ w_in
    split_at = np.cumsum(IN_SPLITS)[:-1].tolist()
    aq, ak, av, gq, gk, gv, gr, zf, zb = jnp.split(proj, split_at, axis=-1)

    def heads(t, nh):
        return t.reshape(B, S, nh, -1)

    aq = apply_partial_rope(heads(aq, ATTN_HEADS))
    ak = apply_partial_rope(heads(ak, ATTN_HEADS))
    ao = dilated_attention(aq, ak, heads(av, ATTN_HEADS)).reshape(B, S, ATTN_WIDTH)
    ao = rmsnorm(ao, attn_norm_g)

    q = heads(gq, GLA_HEADS).astype(f32) * (GLA_DK ** -0.5)
    k = heads(gk, GLA_HEADS).astype(f32)
    v = heads(gv, GLA_HEADS).astype(f32)
    log_gf = jax.nn.log_sigmoid((zf @ gf_up + gf_b).astype(f32)) / GLA_GATE_NORMALIZER
    log_gb = jax.nn.log_sigmoid((zb @ gb_up + gb_b).astype(f32)) / GLA_GATE_NORMALIZER
    flip = lambda t: jnp.flip(t, axis=1)
    o_f = gla_chunked(q, k, v, heads(log_gf, GLA_HEADS))
    o_b = flip(gla_chunked(flip(q), flip(k), flip(v), flip(heads(log_gb, GLA_HEADS))))
    go = rmsnorm(o_f + o_b, gla_norm_g).astype(h.dtype)
    go = (go * jax.nn.silu(heads(gr, GLA_HEADS))).reshape(B, S, GLA_VALUE_WIDTH)

    return jnp.concatenate([ao, go], axis=-1) @ w_out

def conv_glu_ffn(h, w_gate, w_up, conv_w, conv_b, w_down):
    gate = h @ w_gate
    gate = lax.conv_general_dilated(
        gate, conv_w[:, None, :].astype(gate.dtype), window_strides=(1,),
        padding=((CONV_WIDTH // 2, CONV_WIDTH // 2),),
        dimension_numbers=('NWC', 'WIO', 'NWC'), feature_group_count=D_FF) + conv_b
    return (jax.nn.silu(gate) * (h @ w_up)) @ w_down

def setup_inputs(seed: int = 0) -> dict:
    key = jax.random.key(seed)
    ks = jax.random.split(key, 20)
    nrm = lambda k, shape, scale: jax.random.normal(k, shape, jnp.float32) * scale
    gain = lambda k, shape: 1.0 + 0.02 * jax.random.normal(k, shape, jnp.float32)
    L = DEPTH
    return {
        "x": jax.random.normal(ks[0], (BATCH, SEQ, D_MODEL), jnp.float32),
        "norm1_g": gain(ks[1], (L, D_MODEL)),
        "w_in": nrm(ks[2], (L, D_MODEL, IN_WIDTH), D_MODEL ** -0.5),
        "gf_up": nrm(ks[3], (L, GLA_GATE_RANK, GLA_KEY_WIDTH), GLA_GATE_RANK ** -0.5),
        "gf_b": nrm(ks[4], (L, GLA_KEY_WIDTH), 0.1),
        "gb_up": nrm(ks[5], (L, GLA_GATE_RANK, GLA_KEY_WIDTH), GLA_GATE_RANK ** -0.5),
        "gb_b": nrm(ks[6], (L, GLA_KEY_WIDTH), 0.1),
        "gla_norm_g": gain(ks[7], (L, GLA_DV)),
        "attn_norm_g": gain(ks[8], (L, ATTN_WIDTH)),
        "w_out": nrm(ks[9], (L, D_MODEL, D_MODEL), D_MODEL ** -0.5),
        "norm2_g": gain(ks[10], (L, D_MODEL)),
        "w_gate": nrm(ks[11], (L, D_MODEL, D_FF), D_MODEL ** -0.5),
        "w_up": nrm(ks[12], (L, D_MODEL, D_FF), D_MODEL ** -0.5),
        "conv_w": nrm(ks[13], (L, CONV_WIDTH, D_FF), CONV_WIDTH ** -0.5),
        "conv_b": nrm(ks[14], (L, D_FF), 0.02),
        "w_down": nrm(ks[15], (L, D_FF, D_MODEL), D_FF ** -0.5),
        "final_norm_g": gain(ks[16], (D_MODEL,)),
    }

def reference(x, norm1_g, w_in, gf_up, gf_b, gb_up, gb_b, gla_norm_g, attn_norm_g, w_out,
              norm2_g, w_gate, w_up, conv_w, conv_b, w_down, final_norm_g):
    h = x
    for l in range(DEPTH):
        h = h + hybrid_mixer(rmsnorm(h, norm1_g[l]), w_in[l], gf_up[l], gf_b[l], gb_up[l], gb_b[l],
                             gla_norm_g[l], attn_norm_g[l], w_out[l])
        h = h + conv_glu_ffn(rmsnorm(h, norm2_g[l]), w_gate[l], w_up[l], conv_w[l], conv_b[l], w_down[l])
    return rmsnorm(h, final_norm_g)


_drawn_inputs = setup_inputs


def setup_inputs(seed=0):
    import zlib

    import numpy as np

    out = dict(_drawn_inputs(seed))
    spreads = {}
    factors = {'gf_b': 5.427,
     'gb_b': 5.282,
     'gla_norm_g': 7.73,
     'attn_norm_g': 5.004,
     'norm2_g': 4.596,
     'conv_b': 6.678,
     'final_norm_g': 2.912}
    for name, (base, spread) in spreads.items():
        noise = np.random.default_rng([zlib.crc32(name.encode()), seed]).standard_normal(out[name].shape)
        drawn = base * np.exp(spread * noise) if base else spread * noise
        out[name] = __import__('jax').numpy.asarray(drawn.astype(out[name].dtype))
    for name, factor in factors.items():
        out[name] = (out[name] * factor).astype(out[name].dtype)
    return out
```

```python
from contextlib import ExitStack

import concourse.bass as bass
import numpy as np
from concourse import mybir

F32 = mybir.dt.float32
F32R = mybir.dt.float32r
I32 = mybir.dt.int32
ALU = mybir.AluOpType
ACT = mybir.ActivationFunctionType
AX_X = mybir.AxisListType.X

P = 128
S = 512
D = 2048
ST = S // P
KT = D // P
EPS = 1e-6

AW = 1024
AH = 8
HD = AW // AH
ROPE = HD // 4
PATTERNS = ((128, 1), (512, 4), (2048, 16))
THETA = 500000.0
ASCALE = float(HD) ** -0.5

GH = 4
GK = 512
GV = 1024
DK = GK // GH
DV = GV // GH
RANK = 16
CH = 64
NC = S // CH
GSCALE = float(DK) ** -0.5

F = 5632
FT = F // P
G = 4
NG = FT // G

OFF_AQ, OFF_AK, OFF_AV = 0, AW, 2 * AW
OFF_GQ = 3 * AW
OFF_GK, OFF_GV = OFF_GQ + GK, OFF_GQ + 2 * GK
OFF_GR = OFF_GV + GV
OFF_Z = OFF_GR + GV
IN_W = OFF_Z + 2 * RANK

BLK = 512
KS = 2
SLAB = KS * BLK
NSL = KT // KS

IN_BLOCKS = [("gq", OFF_GQ, "f"), ("gk", OFF_GK, "f"), ("gr0", OFF_GR, "f"), ("gr1", OFF_GR + BLK, "f"),
             ("gv0", OFF_GV, "t"), ("gv1", OFF_GV + BLK, "t"),
             ("aq0", OFF_AQ, "f"), ("ak0", OFF_AK, "f"), ("av0", OFF_AV, "t"),
             ("aq1", OFF_AQ + BLK, "f"), ("ak1", OFF_AK + BLK, "f"), ("av1", OFF_AV + BLK, "t")]
Z_SLABS = 2
Z_COL = IN_W - P
Z_KS = KT // Z_SLABS
IN0 = Z_SLABS
WG0 = IN0 + NSL * len(IN_BLOCKS)
HALF = NSL // 2
WA0 = WG0 + HALF * (D // BLK)
FF0 = WA0 + HALF * (D // BLK)
GROUP = 2 * NSL + 2 * (D // BLK)
RING = 3

START = {name: IN0 + NSL * b for b, (name, _, _) in enumerate(IN_BLOCKS)}


def side_pieces():
    side = {}

    def put(n, piece, arg):
        side.setdefault(n, []).append((piece, arg))

    first = START["gv0"] + 4
    for hd in range(2 * GH):
        n = first + 4 * hd
        put(n, "gate", hd)
        put(n + 1, "decay", hd)
        put(n + 2, "keys", hd)
        put(n + 4, "states_a", hd)
        put(n + 4, "states_b", hd)
        put(n + 5, "gla_out", hd)
        if hd % 2:
            put(n + 6, "gla_norm", hd // 2)
    for h in range(AH // 2):
        n = START["aq1"] + 6 * h
        for k, piece in enumerate(("scores", "pnorm", "ptrans", "pv")):
            put(n + k, piece, h)
    for i in range(HALF):
        put(START["av1"] + i + 1, "gla_cat", i)
    for h in range(AH // 2, AH):
        n = WG0 + 4 * (h - AH // 2)
        for k, piece in enumerate(("scores", "pnorm", "ptrans", "pv")):
            put(n + k, piece, h)
    put(WA0 - 1, "attn_cat", 0)
    rank = {p: r for r, p in enumerate(("gla_norm", "gla_out", "states_a", "states_b", "keys", "decay", "gate"))}
    return {n: sorted(v, key=lambda x: rank.get(x[0], 99)) for n, v in side.items()}


SIDE = side_pieces()
NROWS = 2 * KT + AH + 2
G_N1, G_N2, G_AN, G_GN = 0, KT, 2 * KT, 2 * KT + AH
PCOLS = NROWS + 4 * FT
TAP = [NROWS + k * FT for k in range(3)]
CBIAS = NROWS + 3 * FT
TOEP = 2 * S - P


def constant_tables():
    t = np.arange(P)
    same = (t[:, None] // CH) == (t[None, :] // CH)
    sums, masks = [], []
    for back in (False, True):
        seen = same & ((t[:, None] >= t[None, :]) if back else (t[:, None] <= t[None, :]))
        b = seen.astype(np.float64) / 16.0
        start = t // CH * CH
        ref = start + (CH // 2 if back else CH // 2 - 1)
        last = start + (0 if back else CH - 1)
        sums += [b - b[:, ref], b, b[:, last] - b]
        masks.append(seen.astype(np.int32))
    x = np.arange(TOEP)[None, :] - (S - P) - t[:, None]
    count = np.zeros(x.shape)
    for window, d in PATTERNS:
        count += (x % d == 0) & (np.abs(x) <= window // 2)
    toep = np.where(count > 0, np.log(np.maximum(count, 1)) / ASCALE, -1e30)
    floats = np.concatenate([np.eye(P)] + sums, axis=1).astype(np.float32)
    half = ROPE // 2
    ang = (np.float32(THETA) ** (-np.arange(0, ROPE, 2, dtype=np.float32) / np.float32(ROPE)))[:, None] \
        * np.arange(S, dtype=np.float32)[None, :]
    ang = ang.astype(np.float32).astype(np.float64)
    cos, sin = np.cos(ang), np.sin(ang)
    rope = np.concatenate([np.concatenate([cos, cos], 0), np.concatenate([-sin, sin], 0)], axis=1)
    assert rope.shape == (2 * half, 2 * S)
    return floats, toep.astype(np.float32), rope.astype(np.float32), np.concatenate(masks, axis=1)


def encoder_block(nc, x, norm1_g, w_in, gf_up, gf_b, gb_up, gb_b, gla_norm_g, attn_norm_g, w_out,
                  norm2_g, w_gate, w_up, conv_w, conv_b, w_down, final_norm_g, tables, toep, rope, masks, out):
    ctx = ExitStack()
    cursor = [(nc.sbuf_base + 31) // 32 * 32]

    def at(name, offset, shape, dt):
        return nc.alloc_sbuf_tensor_at(name, shape, dt, offset=offset)

    def sb(name, shape, dt=F32):
        size = int(np.prod(shape[1:])) * 4
        offset = cursor[0]
        cursor[0] += (size + 31) // 32 * 32
        return at(name, offset, shape, dt)

    with ctx:
        def sem(name):
            return ctx.enter_context(nc.semaphore(name))

        xT_hi = sb("xT_hi", [P, KT, S], F32R)
        xT_lo = sb("xT_lo", [P, KT, S], F32R)
        raw = [sb(f"raw{i}", [P, SLAB]) for i in range(RING)]
        w_hi = [sb(f"w_hi{i}", [P, SLAB], F32R) for i in range(RING)]
        w_lo = [sb(f"w_lo{i}", [P, SLAB], F32R) for i in range(RING)]
        tab = sb("tab", [P, 7 * P])
        ident = tab[:, 0:P]
        sums = [tab[:, P * (1 + i):P * (2 + i)] for i in range(6)]
        seen = sb("seen", [P, 2 * P], I32)
        ones = sb("ones", [P, P])
        small = sb("small", [P, 2 * S])
        zrope = sb("zrope", [P, S])
        par = sb("par", [P, PCOLS])
        stat = sb("stat", [P, 64])
        gpar = sb("gpar", [P, 4, G])
        KB = 1024
        arena = cursor[0]
        assert arena + 94 * KB <= nc.sbuf_top, (arena, nc.sbuf_top)

        def ar(name, kb, shape, dt=F32):
            return at(name, arena + int(kb * KB), shape, dt)

        xin = [ar(f"xin{s}", 8 * s, [P, D]) for s in range(ST)]
        junk = ar("junk", 64, [P, D])
        prow = ar("prow", 32, [P, 5, P])
        gq = ar("gq", 0, [P, GH, S])
        gk = ar("gk", 8, [P, GH, S])
        gv = ar("gv", 16, [P, ST, GV])
        go = ar("go", 32, [P, 2 * GH, S])
        qT = [ar("qT0", 48, [P, 4, S]), ar("qT1", 8, [P, 4, S])]
        kT = [ar("kT0", 56, [P, 4, S]), ar("kT1", 16, [P, 4, S])]
        vv = [ar("vv0", 0, [P, ST, BLK]), ar("vv1", 24, [P, ST, BLK])]
        e = [ar(f"e{i}", 64 + 2 * i, [P, S]) for i in range(4)]
        state = ar("state", 72, [P, NC, DV])
        osq = ar("osq", 72, [P, 2, S])
        kst = ar("kst", 80, [P, ST, P])
        at_m = [ar(f"at_m{i}", 82 + 2 * i, [P, ST, P]) for i in range(2)]
        gg = ar("gg", 86, [P, ST, P])
        gt = ar("gt", 88, [P, S])
        o_acc = ar("o_acc", 90, [P, 2, S])
        prob = ar("prob", 64, [P, ST, S])
        probT = ar("probT", 72, [P, ST, S])
        offs = ar("offs", 80, [P, TOEP])
        sq = ar("sq", 84, [P, S])
        sqsum = ar("sqsum", 86, [P, S])
        rbc = ar("rbc", 88, [P, S])
        vcat = [ar(f"vcat{i}", 90 + 2 * i, [P, S]) for i in range(2)]
        hid = [ar("hid0", 56, [P, ST, BLK]), ar("hid1", 0, [P, ST, BLK]),
               ar("hid2", 32, [P, ST, BLK]), ar("hid3", 40, [P, ST, BLK])]
        act_hi = ar("act_hi", 16, [P, G, S], F32R)
        act_lo = ar("act_lo", 24, [P, G, S], F32R)
        cv = ar("cv", 64, [P, G, S])
        hn = [ar(f"hn{i}", 72 + 2 * i, [P, ST, P]) for i in range(2)]
        sqj = ar("sqj", 76, [P, BLK])
        gfin = ar("gfin", 78, [P, D])

        acc = [ctx.enter_context(nc.psum_tensor(f"acc{i}", [P, BLK], F32)) for i in range(8)]
        A, B = acc[:4], acc[4:]

        SSQ, RSTD, SS2, MX, NMX, DEN, RDEN, DEC = 0, 4, 8, 24, 28, 32, 36, 40

        tab_in = sem("tab_in")
        offs_in = sem("offs_in")
        x_in = [sem(f"x_in{s}") for s in range(ST)]
        w_in_sem = [sem(f"w_landed{i}") for i in range(RING)]
        hi_done = sem("hi_done")
        lo_done = sem("lo_done")
        slab_done = sem("slab_done")
        bank_done = sem("bank_done")
        hid_added = sem("hid_added")
        act_chain = sem("act_chain")
        dve_chain = sem("dve_chain")
        pool_init = sem("pool_init")
        pool_chain = sem("pool_chain")
        par_t = sem("par_t")
        par_done = sem("par_done")
        ssq_done = sem("ssq_done")
        inv_done = sem("inv_done")
        rstd_done = sem("rstd_done")
        xn_done = sem("xn_done")
        turned = sem("turned")
        xhi_done = sem("xhi_done")
        x_ready = sem("x_ready")
        gate_pre = sem("gate_pre")
        l_done = sem("l_done")
        g_done = sem("g_done")
        decay_done = sem("decay_done")
        exp_done = sem("exp_done")
        keys_done = sem("keys_done")
        kst_t = sem("kst_t")
        kst_done = sem("kst_done")
        at_done = sem("at_done")
        at_masked = sem("at_masked")
        kv_done = sem("kv_done")
        kv_used = sem("kv_used")
        o_done = sem("o_done")
        o_saved = sem("o_saved")
        osq_done = sem("osq_done")
        osum_done = sem("osum_done")
        oinv_done = sem("oinv_done")
        orstd_done = sem("orstd_done")
        go_done = sem("go_done")
        in_act = sem("in_act")
        rope_done = sem("rope_done")
        score_done = sem("score_done")
        max_done = sem("max_done")
        p_exp = sem("p_exp")
        p_done = sem("p_done")
        p_turned = sem("p_turned")
        pt_act = sem("pt_act")
        pt_dve = sem("pt_dve")
        pv_done = sem("pv_done")
        oT_done = sem("oT_done")
        sqsum_done = sem("sqsum_done")
        cat_v = sem("cat_v")
        cat_hi = sem("cat_hi")
        hid_in = [sem(f"hid_in{j}") for j in range(4)]
        hn_done = sem("hn_done")
        conv1 = sem("conv1")
        conv2 = sem("conv2")
        silu_done = sem("silu_done")
        act_done = sem("act_done")
        ahi_done = sem("ahi_done")
        alo_done = sem("alo_done")
        fsq_done = sem("fsq_done")
        fin_done = sem("fin_done")
        stored = sem("stored")
        gpar_done = sem("gpar_done")
        conv_first = sem("conv_first")

        w_in_t = w_in.rearrange("l (t p) n -> p (l t) n", p=P)
        w_out_t = w_out.rearrange("l (t p) n -> p (l t) n", p=P)
        w_gate_t = w_gate.rearrange("l (t p) n -> p (l t) n", p=P)
        w_up_t = w_up.rearrange("l (t p) n -> p (l t) n", p=P)
        w_down_t = w_down.rearrange("l (t p) n -> p (l t) n", p=P)
        x_t = x.rearrange("b (s p) n -> p (b s) n", p=P)
        out_t = out.rearrange("b (s p) n -> p (b s) n", p=P)

        def mixer_slab(n):
            if n < IN0:
                return w_in_t[:, Z_KS * n:Z_KS * (n + 1), Z_COL:Z_COL + P]
            if n < WG0:
                b, i = divmod(n - IN0, NSL)
                c = IN_BLOCKS[b][1]
                return w_in_t[:, KS * i:KS * (i + 1), c:c + BLK]
            b, i = divmod(n - WG0, HALF)
            t = KS * i + (KT // 2 if n < WA0 else 0)
            j = b % (D // BLK)
            return w_out_t[:, t:t + KS, j * BLK:(j + 1) * BLK]

        ORDER = [("gate", i) for i in range(NSL)] + [("down", i) for i in range(2 * (D // BLK))] \
            + [("up", i) for i in range(NSL)]
        FIRST = [w for w in ORDER if w[0] != "down"]
        LAST = [w for w in ORDER if w[0] == "down"]
        LOOP0 = FF0 + len(FIRST)
        LAST0 = LOOP0 + (NG - 1) * GROUP
        assert GROUP % RING == 0

        def ffn_slab(what, i, g):
            if what == "down":
                j, half = divmod(i, 2)
                src = w_down_t[:, bass.ds((g - 1) * G + half * KS, KS), j * BLK:(j + 1) * BLK]
                return src
            src = w_gate_t if what == "gate" else w_up_t
            return src[:, KS * i:KS * (i + 1), bass.ds(g * BLK, BLK)]

        def ksplit(t, n):
            return t.rearrange("p (k c) -> p k c", c=n)

        def bank_base(what, j, g, step):
            mixer = 3 * (len(IN_BLOCKS) + 2 * (D // BLK))
            per = 3 * (2 + D // BLK)
            if not step:
                return mixer + (0 if what == "gate" else 3)
            start = mixer + 6 + (g - 1) * per
            if what == "gate":
                return start
            if what == "down":
                return start + 3 + 3 * j
            return start + 3 + 3 * (D // BLK)

        block = ctx.enter_context(nc.Block())

        @block.sync
        def _(sp):
            def load(n0, src, g=0, step=0):
                slot = n0 % RING
                c = src.shape[2]
                if n0 >= RING or step:
                    sp.wait_ge(lo_done, n0 - RING + 1 + step * g)
                sp.dma_start(ksplit(raw[slot][:, :], c), src).then_inc(w_in_sem[slot], 16)

            for s in range(ST):
                sp.dma_start(xin[s][:, :], x_t[:, s, :]).then_inc(x_in[s], 16)
            for n in range(FF0):
                load(n, mixer_slab(n))
            for i, (what, k) in enumerate(FIRST):
                load(FF0 + i, ffn_slab(what, k, 0))
            with sp.Fori(1, NG) as g:
                for i, (what, k) in enumerate(ORDER):
                    load(LOOP0 - GROUP + i, ffn_slab(what, k, g), g, GROUP)
            for i, (what, k) in enumerate(LAST):
                load(LAST0 + i, ffn_slab(what, k, NG))
            for j in range(4):
                for s in range(ST):
                    sp.wait_ge(fin_done, 4 * j + s + 1)
                    sp.dma_start(out_t[:, s, j * BLK:(j + 1) * BLK], hid[j][:, s, :]).then_inc(stored, 16)
            sp.wait_ge(stored, 16 * 16)

        @block.gpsimd
        def _(pool):
            for n, (view, value) in enumerate(((ones[:, :], 1.0), (small[64:96, :], 0.0), (zrope[64:96, :], 0.0),
                                               (zrope[64:65, :], 1.0), (small[96:128, :], 0.0))):
                pool.memset(view, value).then_inc(pool_init, 1)
                pool.wait_ge(pool_init, n + 1)
            pool.dma_start(tab[:, :], tables).then_inc(tab_in, 16)
            pool.dma_start(seen[:, :], masks).then_inc(tab_in, 16)
            pool.dma_start(small[0:ROPE, :], rope).then_inc(tab_in, 16)
            for d, (up, bias) in enumerate(((gf_up, gf_b), (gb_up, gb_b))):
                pool.dma_start(small[64:65, d * GK:(d + 1) * GK], bias).then_inc(tab_in, 16)
                pool.dma_start(small[96 + RANK * d:96 + RANK * (d + 1), d * GK:(d + 1) * GK], up[0])\
                    .then_inc(tab_in, 16)
            rows = [(norm1_g, G_N1), (norm2_g, G_N2), (attn_norm_g, G_AN), (gla_norm_g, G_GN)]
            for src, r in rows:
                k = src.shape[1] // P
                pool.dma_start(prow[r:r + k, 0, :], src.rearrange("l (r c) -> (l r) c", c=P)).then_inc(tab_in, 16)
            for k in range(3):
                pool.dma_start(prow[0:FT, 1 + k, :], conv_w[0, k, :].rearrange("(r c) -> r c", c=P))\
                    .then_inc(tab_in, 16)
            pool.dma_start(prow[0:FT, 4, :], conv_b.rearrange("l (r c) -> (l r) c", c=P)).then_inc(tab_in, 16)

            pool.wait_ge(xn_done, ST)
            for i in range(2):
                pool.memset(at_m[i][:, :, :], 0.0).then_inc(pool_init, 1)
                pool.wait_ge(pool_init, 6 + i)
            pool.wait_ge(go_done, GH)
            pool.dma_start(offs[:, :], toep).then_inc(offs_in, 16)
            for h in range(AH):
                o = qT[h // 4][:, h % 4, :]
                pool.wait_ge(oT_done, h + 1)
                if h == 0:
                    pool.tensor_tensor(sqsum[:, :], o, o, ALU.mult).then_inc(sqsum_done, 1)
                else:
                    pool.wait_ge(sqsum_done, h)
                    pool.tensor_tensor(sq[:, :], o, o, ALU.mult).then_inc(pool_chain, 1)
                    pool.wait_ge(pool_chain, h)
                    pool.tensor_tensor(sqsum[:, :], sqsum[:, :], sq[:, :], ALU.add).then_inc(sqsum_done, 1)
                if h == 3:
                    pool.wait_ge(x_ready, KT + 2 * GH)
                    for j in range(4):
                        pool.dma_start(hid[j][:, :, :], x_t[:, :, j * BLK:(j + 1) * BLK]).then_inc(hid_in[j], 16)
            pool.wait_ge(x_ready, 3 * KT)
            pool.dma_start(gfin[:, :], final_norm_g.partition_broadcast(P)).then_inc(offs_in, 16)

        n_tab = 16 * (3 + 4 + 4 + 4)

        IN_BANKS = 1 + 4 * len(IN_BLOCKS)
        OUT_BANKS = 4 * 2 * (D // BLK)
        DOWN_BANKS = 4 * (D // BLK)

        @block.tensor
        def _(pe):
            def three(o, wh, wl, ah, al, first, last, weights_first):
                for k, (w, a) in enumerate(((wh, ah), (wh, al), (wl, ah))):
                    lhs, rhs = (w, a) if weights_first else (a, w)
                    mm = pe.matmul(o, lhs, rhs, start=first and k == 0, stop=last and k == 2)
                return mm

            def slab(n0, wait, kind, banks, k0, first, last, free=None, inputs=(xT_hi, xT_lo)):
                slot = n0 % RING
                pe.wait_ge(lo_done, wait + 1)
                hi, lo = ksplit(w_hi[slot][:, :], BLK), ksplit(w_lo[slot][:, :], BLK)
                for m in range(4):
                    if first:
                        free(m)
                    c = slice(m * P, (m + 1) * P)
                    for k in range(KS):
                        a, al = inputs[0][:, k0 + k], inputs[1][:, k0 + k]
                        if kind == "f":
                            wh, wl = hi[:, k, c], lo[:, k, c]
                        else:
                            wh, wl, a, al = hi[:, k, :], lo[:, k, :], a[:, c], al[:, c]
                        mm = three(banks[m][:, :], wh, wl, a, al, first and k == 0, last and k == KS - 1, kind == "f")
                    if m == 3:
                        mm.then_inc(slab_done, 1)
                    elif last:
                        mm.then_inc(bank_done, 1)

            pe.wait_ge(tab_in, n_tab)
            pe.wait_ge(pool_init, 5)
            for k in range(5):
                r, c = (NROWS, 0) if k == 0 else (FT, NROWS + (k - 1) * FT)
                mm = pe.transpose(B[0][:, c:c + r], prow[0:r, k, :], ident[0:r, 0:r])
            mm.then_inc(par_t, 1)

            def turn_tile(k, src, seq):
                if seq >= 4:
                    pe.wait_ge(x_ready, seq - 3)
                for s in range(ST):
                    mm = pe.transpose(B[k % 4][:, s * P:(s + 1) * P], src(s), ident)
                mm.then_inc(turned, 1)

            pe.wait_ge(xn_done, ST)
            pe.wait_ge(par_done, 1)
            for k in range(KT):
                turn_tile(k, lambda s: xin[s][:, k * P:(k + 1) * P], k)

            def gate(hd):
                h, d = divmod(hd, 2)
                if hd:
                    pe.wait_ge(kv_used, 2 * hd)
                if hd == 0:
                    pe.wait_ge(in_act, 1)
                w = small[64:P, d * GK + h * DK:d * GK + (h + 1) * DK]
                for t in range(ST):
                    mm = pe.matmul(B[3][:, t * P:(t + 1) * P], zrope[64:P, t * P:(t + 1) * P], w, start=True, stop=True)
                mm.then_inc(gate_pre, 1)

            def decay(hd):
                d = hd % 2
                pe.wait_ge(g_done, hd + 1)
                if hd:
                    pe.wait_ge(o_saved, hd)
                for i, b in ((1, 2), (2, 3), (0, 1)):
                    for t in range(ST):
                        mm = pe.matmul(B[b][:, t * P:(t + 1) * P], gg[:, t, :], sums[3 * d + i], start=True, stop=True)
                mm.then_inc(decay_done, 1)

            def keys(hd):
                pe.wait_ge(keys_done, hd + 1)
                for t in range(ST):
                    mm = pe.transpose(B[0][:, t * P:(t + 1) * P], e[3][:, t * P:(t + 1) * P], ident)
                mm.then_inc(kst_t, 1)
                for t in range(ST):
                    c = slice(t * P, (t + 1) * P)
                    mm = pe.matmul(B[1][:, c], e[1][:, c], e[0][:, c], start=True, stop=True)
                mm.then_inc(at_done, 1)

            def states(hd, part):
                h, d = divmod(hd, 2)
                if part == 0:
                    pe.wait_ge(kst_done, hd + 1)
                    pe.wait_ge(in_act, 1 + 4 * (5 + h // 2))
                    if d == 0 and h:
                        pe.wait_ge(oinv_done, h)
                else:
                    pe.wait_ge(kv_used, 2 * hd + 1)
                for i in range(4 - part):
                    step = 4 * part + i
                    c = NC - 1 - step if d else step
                    r = (c % 2) * CH
                    o = B[2 + c % 2][:, (i // 2) * DV:(i // 2 + 1) * DV]
                    mm = pe.matmul(o, kst[r:r + CH, c // 2, :], gv[r:r + CH, c // 2, h * DV:(h + 1) * DV],
                                   start=True, stop=True)
                mm.then_inc(kv_done, 1)

            def gla_out(hd):
                h, d = divmod(hd, 2)
                pe.wait_ge(at_masked, hd + 1)
                pe.wait_ge(kv_used, 2 * hd + 2)
                for v in range(2):
                    for t in range(ST):
                        c = slice(t * P, (t + 1) * P)
                        pe.matmul(B[v][:, c], gv[:, t, h * DV + v * P:h * DV + (v + 1) * P],
                                  at_m[d][:, t, :], start=(t == 0), stop=False, skip_group_check=True)
                    for c in range(NC - 1):
                        c = c if d else c + 1
                        mm = pe.matmul(B[v][:, c * CH:(c + 1) * CH], state[:, c, v * P:(v + 1) * P],
                                       e[2][:, c * CH:(c + 1) * CH], start=False, stop=True, skip_group_check=True)
                mm.then_inc(o_done, 1)

            def gla_norm(h):
                pe.wait_ge(osq_done, h + 1)
                nxt = 2 * h + 2
                if nxt < 2 * GH:
                    pe.wait_ge(exp_done, nxt + 1)
                for v in range(2):
                    mm = pe.matmul(B[3][:, :], ones[:, :], osq[:, v, :], start=(v == 0), stop=(v == 1))
                mm.then_inc(osum_done, 1)

            def scores(h):
                b, hh = divmod(h, 4)
                pe.wait_ge(rope_done, 2 * b + 2)
                if h == 0:
                    pe.wait_ge(oinv_done, GH)
                    pe.wait_ge(o_saved, 2 * GH)
                else:
                    pe.wait_ge(oT_done, h)
                    pe.wait_ge(pt_dve, 2 * h)
                for t in range(ST):
                    pe.matmul(B[t][:, :], qT[b][:, hh, t * P:(t + 1) * P], kT[b][:, hh, :], start=True, stop=True)\
                        .then_inc(score_done, 1)

            def ptrans(h):
                pe.wait_ge(p_done, h + 1)
                for j in range(ST):
                    for t in range(ST):
                        mm = pe.transpose(B[j][:, t * P:(t + 1) * P], prob[:, t, j * P:(j + 1) * P], ident)
                    mm.then_inc(p_turned, 1)

            def pv(h):
                b, hh = divmod(h, 4)
                pe.wait_ge(pt_act, 2 * h + 2)
                pe.wait_ge(pt_dve, 2 * h + 2)
                if hh == 0:
                    pe.wait_ge(in_act, 1 + 4 * (9 if b == 0 else 12))
                for j in range(ST):
                    mm = pe.matmul(B[0][:, :], vv[b][:, j, hh * HD:(hh + 1) * HD], probT[:, j, :],
                                   start=(j == 0), stop=(j == ST - 1))
                mm.then_inc(pv_done, 1)

            def attn_cat(_):
                pe.wait_ge(sqsum_done, AH)
                pe.matmul(B[1][:, :], ones[:, :], sqsum[:, :], start=True, stop=True).then_inc(osum_done, 1)

            pieces = {"gate": gate, "decay": decay, "keys": keys, "gla_out": gla_out, "gla_norm": gla_norm,
                      "states_a": lambda hd: states(hd, 0), "states_b": lambda hd: states(hd, 1),
                      "scores": scores, "ptrans": ptrans, "pv": pv, "attn_cat": attn_cat}

            for n in range(FF0):
                if n < IN0:
                    pe.wait_ge(lo_done, n + 1)
                    hi, lo = ksplit(w_hi[n][:, :], P), ksplit(w_lo[n][:, :], P)
                    for k in range(Z_KS):
                        kk = Z_KS * n + k
                        pe.wait_ge(x_ready, kk + 1)
                        mm = three(A[0][:, :], hi[:, k, :], lo[:, k, :], xT_hi[:, kk, :], xT_lo[:, kk, :],
                                   kk == 0, kk == KT - 1, True)
                    mm.then_inc(slab_done, 1)
                elif n < WG0:
                    b, i = divmod(n - IN0, NSL)

                    def in_free(m):
                        pe.wait_ge(in_act, 1 + 4 * (b - 1) + m + 1 if b else 1)

                    slab(n, n, IN_BLOCKS[b][2], A, KS * i, i == 0, i == NSL - 1, in_free)
                else:
                    b, i = divmod(n - WG0, HALF)
                    k0 = KS * i + (0 if n < WA0 else KT // 2)
                    pe.wait_ge(x_ready, KT + k0 + KS)

                    def out_free(m):
                        if b == 0:
                            pe.wait_ge(in_act, IN_BANKS - 3 + m)
                        else:
                            pe.wait_ge(hid_added, 4 * (b - 1) + m + 1)

                    slab(n, n, "t", A, k0, i == 0, i == HALF - 1, out_free)
                for piece, arg in SIDE.get(n, ()):
                    if piece in pieces:
                        pieces[piece](arg)

            for k in range(KT):
                pe.wait_ge(hn_done, k + 1)
                turn_tile(k, lambda s: hn[k % 2][:, s, :], 2 * KT + k)

            def ffn(order, n0, g, step, opening):
                added = OUT_BANKS + DOWN_BANKS * (g - 1)
                for i, (what, k) in enumerate(order):
                    n = n0 + i + step * g
                    if what == "down":
                        j, half = divmod(k, 2)
                        if k == 0:
                            pe.wait_ge(alo_done, G * g)

                        def free(m):
                            if j == 0:
                                pe.wait_ge(act_done, G * (g - 1) + m + 1)
                            elif j == 1 and opening == "last":
                                pe.wait_ge(hid_added, added - 4 + m + 1)
                            elif j == 1:
                                pe.wait_ge(conv2, G * g + m + 1)
                            else:
                                pe.wait_ge(hid_added, added + 4 * (j - 2) + m + 1)

                        slab(n0 + i, n, "t", B if j % 2 == 0 else A, half * KS, half == 0, half == 1, free,
                             (act_hi, act_lo))
                    elif what == "gate":
                        if opening == "first":
                            pe.wait_ge(x_ready, 2 * KT + KS * (k + 1))

                        def free(m):
                            if opening == "first":
                                pe.wait_ge(hid_added, OUT_BANKS - 4 + m + 1)
                            else:
                                pe.wait_ge(conv2, G * (g - 1) + m + 1)
                                pe.wait_ge(hid_added, added - 4 + m + 1)

                        slab(n0 + i, n, "f", A, KS * k, k == 0, k == NSL - 1, free)
                    else:
                        def free(m):
                            if opening == "first":
                                pe.wait_ge(x_ready, 3 * KT)
                            else:
                                pe.wait_ge(hid_added, added + 8 + m + 1)

                        slab(n0 + i, n, "f", B, KS * k, k == 0, k == NSL - 1, free)

            ffn(FIRST, FF0, 0, 0, "first")
            with pe.Fori(1, NG) as g:
                ffn(ORDER, LOOP0 - GROUP, g, GROUP, "loop")
            ffn(LAST, LAST0, NG, 0, "last")

        @block.scalar
        def _(act):
            chain = [0]

            def link(ins):
                chain[0] += 1
                ins.then_inc(act_chain, 1)
                act.wait_ge(act_chain, chain[0])

            def split(n0, wait, g8):
                slot = n0 % RING
                act.wait_ge(w_in_sem[slot], 16 * (n0 // RING + 1) + 16 * g8)
                if n0 >= RING:
                    act.wait_ge(slab_done, wait - RING + 1)
                act.activation(w_hi[slot][:, :], raw[slot][:, :], ACT.Copy).then_inc(hi_done, 1)

            split(0, 0, 0)
            split(1, 1, 0)
            for s in range(ST):
                act.wait_ge(x_in[s], 16)
                if s:
                    act.wait_ge(ssq_done, s)
                act.activation(junk[:, :], xin[s][:, :], ACT.Square, accum_out=stat[:, SSQ + s:SSQ + s + 1])\
                    .then_inc(ssq_done, 1)
            act.wait_ge(inv_done, 1)
            act.activation(stat[:, RSTD:RSTD + ST], stat[:, RSTD:RSTD + ST], ACT.Sqrt).then_inc(rstd_done, 1)
            act.wait_ge(par_t, 1)
            act.activation(par[:, :], B[0][:, 0:PCOLS], ACT.Copy).then_inc(par_done, 1)
            act.wait_ge(par_done, 1)

            def tile_hi(k, g0, seq):
                act.wait_ge(turned, seq + 1)
                act.activation(xT_hi[:, k, :], B[k % 4][:, :], ACT.Copy, scale=par[:, g0 + k:g0 + k + 1])\
                    .then_inc(xhi_done, 1)

            for k in range(KT):
                tile_hi(k, G_N1, k)

            def evac_in(n):
                if n == IN0 - 1:
                    act.wait_ge(slab_done, IN0)
                    act.activation(zrope[96:P, :], A[0][96:P, :], ACT.Copy).then_inc(in_act, 1)
                    return
                b, i = divmod(n - IN0, NSL)
                if n < IN0 or n >= WG0 or i != NSL - 1:
                    return
                name = IN_BLOCKS[b][0]
                if name in ("av0", "aq1", "ak1", "av1"):
                    act.wait_ge(go_done, GH)
                for m in range(4):
                    if m == 3:
                        act.wait_ge(slab_done, n + 1)
                    else:
                        act.wait_ge(bank_done, 3 * b + m + 1)
                    src, fn, scale = A[m][:, :], ACT.Copy, 1.0
                    if name == "gq":
                        dst, scale = gq[:, m, :], GSCALE
                    elif name == "gk":
                        dst = gk[:, m, :]
                    elif name[:2] == "gr":
                        dst, fn = go[:, 4 * int(name[2]) + m, :], ACT.Silu
                    elif name[:2] == "gv":
                        v = int(name[2])
                        dst = gv[:, m, v * BLK:(v + 1) * BLK]
                    elif name[:2] == "aq":
                        dst = qT[int(name[2])][:, m, :]
                    elif name[:2] == "ak":
                        dst = kT[int(name[2])][:, m, :]
                    else:
                        dst = vv[int(name[2])][:, m, :]
                    act.activation(dst, src, fn, scale=scale).then_inc(in_act, 1)

            def gate(hd):
                act.wait_ge(gate_pre, hd + 1)
                if hd:
                    act.wait_ge(g_done, hd)
                if hd >= 3:
                    act.wait_ge(go_done, (hd - 1) // 2)
                link(act.activation(gt[:, :], B[3][:, :], ACT.Abs))
                link(act.activation(gt[:, :], gt[:, :], ACT.Exp, scale=-1.0))
                act.activation(gt[:, :], gt[:, :], ACT.Ln, bias=1.0).then_inc(l_done, 1)

            def decay(hd):
                act.wait_ge(decay_done, hd + 1)
                if hd:
                    act.wait_ge(o_done, hd)
                d = hd % 2
                act.activation(e[0][:, :], B[1][:, :], ACT.Exp)
                act.activation(e[1][:, :], B[1][:, :], ACT.Exp, scale=-1.0)
                act.activation(e[2][:, :], B[2][:, :], ACT.Exp)
                last = B[2][:, :].rearrange("p (c t) -> p c t", t=CH)[:, :, 0 if d else CH - 1]
                act.activation(stat[:, DEC:DEC + NC], last, ACT.Exp)
                act.activation(e[3][:, :], B[3][:, :], ACT.Exp).then_inc(exp_done, 1)

            def keys(hd):
                act.wait_ge(kst_t, hd + 1)
                act.activation(kst[:, :, :], B[0][:, :].rearrange("p (t k) -> p t k", k=P), ACT.Copy)\
                    .then_inc(kst_done, 1)

            def gla_out(hd):
                if hd % 2:
                    h = hd // 2
                    act.wait_ge(o_saved, hd + 1)
                    for v in range(2):
                        ins = act.activation(osq[:, v, :], o_acc[:, v, :], ACT.Square)
                    ins.then_inc(osq_done, 1)

            def gla_norm(h):
                act.wait_ge(oinv_done, h + 1)
                act.activation(gt[:, :], gt[:, :], ACT.Sqrt).then_inc(orstd_done, 1)

            def scores(h):
                act.wait_ge(max_done, h + 1)
                for t in range(ST):
                    ins = act.activation(prob[:, t, :], prob[:, t, :], ACT.Exp, bias=stat[:, NMX + t:NMX + t + 1],
                                         accum_out=stat[:, DEN + t:DEN + t + 1])
                ins.then_inc(p_exp, 1)

            def ptrans(h):
                for j in (0, 2):
                    act.wait_ge(p_turned, 4 * h + j + 1)
                    act.activation(probT[:, j, :], B[j][:, :], ACT.Copy).then_inc(pt_act, 1)

            def pv(h):
                act.wait_ge(pv_done, h + 1)
                act.activation(qT[h // 4][:, h % 4, :], B[0][:, :], ACT.Copy).then_inc(oT_done, 1)

            def gla_cat(i):
                act.wait_ge(slab_done, START["av1"] + i + 1)
                for c in (2 * i, 2 * i + 1):
                    act.activation(xT_hi[:, c, :], go[:, c, :], ACT.Copy).then_inc(xhi_done, 1)

            def attn_cat(_):
                act.wait_ge(oinv_done, GH + 1)
                act.activation(rbc[:, :], rbc[:, :], ACT.Sqrt).then_inc(orstd_done, 1)
                act.wait_ge(slab_done, WG0)
                for h in range(AH):
                    act.wait_ge(cat_v, h + 1)
                    act.activation(xT_hi[:, AH + h, :], vcat[h % 2][:, :], ACT.Copy).then_inc(xhi_done, 1)

            pieces = {"gate": gate, "decay": decay, "keys": keys, "gla_out": gla_out, "gla_norm": gla_norm,
                      "scores": scores, "ptrans": ptrans, "pv": pv, "gla_cat": gla_cat, "attn_cat": attn_cat}
            for n in range(FF0):
                split(n + 2, n + 2, 0)
                evac_in(n)
                for piece, arg in SIDE.get(n, ()):
                    if piece in pieces:
                        pieces[piece](arg)
                if n >= WA0 and (n - WA0) % HALF == HALF - 1:
                    j = (n - WA0) // HALF
                    for s in range(ST):
                        act.wait_ge(hid_added, OUT_BANKS // 2 + 4 * j + s + 1)
                        act.activation(sqj[:, :], hid[j][:, s, :], ACT.Square,
                                       accum_out=stat[:, SS2 + 4 * s + j:SS2 + 4 * s + j + 1]).then_inc(ssq_done, 1)
                        act.wait_ge(ssq_done, ST + 4 * j + s + 1)
            act.wait_ge(inv_done, 2)
            act.activation(stat[:, RSTD:RSTD + ST], stat[:, RSTD:RSTD + ST], ACT.Sqrt).then_inc(rstd_done, 1)
            for k in range(KT):
                tile_hi(k, G_N2, KT + k)

            def ffn(order, n0, g, step):
                for i, (what, k) in enumerate(order):
                    n = n0 + i + step * g
                    if not (n0 + i >= LAST0 + len(LAST) - 2 and not step):
                        split(n0 + i + 2, n + 2, (step // RING) * g)
                    if what == "gate" and k == NSL - 1:
                        for m in range(4):
                            act.wait_ge(gpar_done, g + 1)
                            if m == 3:
                                act.wait_ge(slab_done, n + 1)
                            else:
                                act.wait_ge(bank_done, bank_base(what, 0, g, step) + m + 1)
                            if step:
                                act.wait_ge(alo_done, G * g - G + m + 1)
                            act.activation(cv[:, m, :], A[m][:, :], ACT.Identity, bias=gpar[:, 3, m:m + 1],
                                           scale=gpar[:, 1, m:m + 1]).then_inc(conv1, 1)
                        for m in range(4):
                            act.wait_ge(conv2, G * g + m + 1)
                            act.activation(cv[:, m, :], cv[:, m, :], ACT.Silu).then_inc(silu_done, 1)
                    if what == "up" and k == NSL - 1:
                        for m in range(4):
                            act.wait_ge(act_done, G * g + m + 1)
                            act.activation(act_hi[:, m, :], cv[:, m, :], ACT.Copy).then_inc(ahi_done, 1)

            ffn(FIRST, FF0, 0, 0)
            with act.Fori(1, NG) as g:
                ffn(ORDER, LOOP0 - GROUP, g, GROUP)
            ffn(LAST, LAST0, 0, 0)
            for j in range(4):
                for s in range(ST):
                    act.wait_ge(hid_added, OUT_BANKS + DOWN_BANKS * (NG - 1) + 4 * j + s + 1)
                    act.activation(sqj[:, :], hid[j][:, s, :], ACT.Square,
                                   accum_out=stat[:, SS2 + 4 * s + j:SS2 + 4 * s + j + 1]).then_inc(fsq_done, 1)
                    act.wait_ge(fsq_done, 4 * j + s + 1)
            act.wait_ge(inv_done, 3)
            act.activation(stat[:, RSTD:RSTD + ST], stat[:, RSTD:RSTD + ST], ACT.Sqrt).then_inc(rstd_done, 1)

        @block.vector
        def _(dve):
            chain = [0]

            def link(ins):
                chain[0] += 1
                ins.then_inc(dve_chain, 1)
                dve.wait_ge(dve_chain, chain[0])

            def split(n0, wait):
                slot = n0 % RING
                dve.wait_ge(hi_done, wait + 1)
                dve.tensor_tensor(w_lo[slot][:, :], raw[slot][:, :], w_hi[slot][:, :].bitcast(F32), ALU.subtract)\
                    .then_inc(lo_done, 1)

            def inverse(src, dst, width, waited):
                link(dve.tensor_scalar(dst, src, 1.0 / width, EPS, ALU.mult, ALU.add))
                dve.reciprocal(dst, dst).then_inc(waited, 1)

            split(0, 0)
            split(1, 1)
            dve.wait_ge(ssq_done, ST)
            inverse(stat[:, SSQ:SSQ + ST], stat[:, RSTD:RSTD + ST], D, inv_done)
            dve.wait_ge(rstd_done, 1)
            for s in range(ST):
                dve.tensor_scalar(xin[s][:, :], xin[s][:, :], stat[:, RSTD + s:RSTD + s + 1], None, ALU.mult)\
                    .then_inc(xn_done, 1)

            def tile_lo(k, g0, seq):
                dve.wait_ge(xhi_done, seq + 1)
                dve.scalar_tensor_tensor(out=xT_lo[:, k, :], in0=B[k % 4][:, :], scalar=par[:, g0 + k:g0 + k + 1],
                                         in1=xT_hi[:, k, :].bitcast(F32), op0=ALU.mult, op1=ALU.subtract)\
                    .then_inc(x_ready, 1)

            dve.wait_ge(par_done, 1)
            for k in range(KT):
                tile_lo(k, G_N1, k)

            def rotate(block_t, seq):
                swap = [(r + ROPE // 2) % ROPE for r in range(ROPE)]
                for m in range(4):
                    dve.wait_ge(in_act, seq + m + 1)
                    src = block_t[0:ROPE, m, :]
                    link(dve.stream_shuffle(zrope[0:ROPE, :], src, swap))
                    link(dve.tensor_tensor(zrope[0:ROPE, :], zrope[0:ROPE, :], small[0:ROPE, S:2 * S], ALU.mult))
                    link(dve.tensor_tensor(src, src, small[0:ROPE, 0:S], ALU.mult))
                    ins = dve.tensor_tensor(src, src, zrope[0:ROPE, :], ALU.add)
                    if m < 3:
                        link(ins)
                    else:
                        ins.then_inc(rope_done, 1)

            def gate(hd):
                dve.wait_ge(l_done, hd + 1)
                if hd:
                    dve.wait_ge(decay_done, hd)
                dve.scalar_tensor_tensor(out=gg[:, :, :].rearrange("p t k -> p (t k)"), in0=B[3][:, :], scalar=0.0,
                                         in1=gt[:, :], op0=ALU.min, op1=ALU.subtract).then_inc(g_done, 1)

            def decay(hd):
                h = hd // 2
                dve.wait_ge(exp_done, hd + 1)
                dve.wait_ge(in_act, 1 + 8)
                for i, src in enumerate((gq, gk, gq, gk)):
                    ins = dve.tensor_tensor(e[i][:, :], e[i][:, :], src[:, h, :], ALU.mult)
                ins.then_inc(keys_done, 1)

            def keys(hd):
                d = hd % 2
                dve.wait_ge(at_done, hd + 1)
                if hd == 0:
                    dve.wait_ge(pool_init, 7)
                mask = seen[:, d * P:(d + 1) * P]
                for t in range(ST):
                    ins = dve.copy_predicated(at_m[d][:, t, :], mask, B[1][:, t * P:(t + 1) * P])
                ins.then_inc(at_masked, 1)

            def states(hd, part):
                d = hd % 2
                dve.wait_ge(kv_done, 2 * hd + part + 1)
                for i in range(4):
                    step = 4 * part + i
                    c = NC - 1 - step if d else step
                    nxt = c - 1 if d else c + 1
                    kv = B[2 + c % 2][:, (i // 2) * DV:(i // 2 + 1) * DV]
                    if step == 0:
                        link(dve.tensor_copy(state[:, nxt, :], kv))
                    elif step < NC - 1:
                        ins = dve.scalar_tensor_tensor(out=state[:, nxt, :], in0=state[:, c, :],
                                                       scalar=stat[:, DEC + c:DEC + c + 1], in1=kv,
                                                       op0=ALU.mult, op1=ALU.add)
                        if i == 3 or step == NC - 2:
                            ins.then_inc(kv_used, 1)
                            dve.wait_ge(kv_used, 2 * hd + part + 1)
                        else:
                            link(ins)

            def gla_out(hd):
                d = hd % 2
                dve.wait_ge(o_done, hd + 1)
                for v in range(2):
                    if d == 0:
                        ins = dve.tensor_copy(o_acc[:, v, :], B[v][:, :])
                    else:
                        ins = dve.tensor_tensor(o_acc[:, v, :], o_acc[:, v, :], B[v][:, :], ALU.add)
                ins.then_inc(o_saved, 1)

            def gla_norm(h):
                dve.wait_ge(osum_done, h + 1)
                if h < GH - 1:
                    dve.wait_ge(g_done, 2 * h + 3)
                inverse(B[3][:, :], gt[:, :], DV, oinv_done)
                dve.wait_ge(orstd_done, h + 1)
                for v in range(2):
                    link(dve.scalar_tensor_tensor(out=o_acc[:, v, :], in0=o_acc[:, v, :],
                                                  scalar=par[:, G_GN + v:G_GN + v + 1], in1=gt[:, :],
                                                  op0=ALU.mult, op1=ALU.mult))
                    ins = dve.tensor_tensor(go[:, 2 * h + v, :], go[:, 2 * h + v, :], o_acc[:, v, :], ALU.mult)
                ins.then_inc(go_done, 1)

            def scores(h):
                if h == 0:
                    dve.wait_ge(offs_in, 16)
                for t in range(ST):
                    dve.wait_ge(score_done, 4 * h + t + 1)
                    x0 = S - P - t * P
                    ins = dve.tensor_tensor_reduce(out=prob[:, t, :], in0=B[t][:, :], in1=offs[:, x0:x0 + S],
                                                   scale=ASCALE, scalar=-3e38, op0=ALU.add, op1=ALU.max,
                                                   accum_out=stat[:, MX + t:MX + t + 1])
                link(ins)
                dve.tensor_scalar(stat[:, NMX:NMX + ST], stat[:, MX:MX + ST], -1.0, None, ALU.mult)\
                    .then_inc(max_done, 1)

            def pnorm(h):
                dve.wait_ge(p_exp, h + 1)
                link(dve.reciprocal(stat[:, RDEN:RDEN + ST], stat[:, DEN:DEN + ST]))
                for t in range(ST):
                    ins = dve.tensor_scalar(prob[:, t, :], prob[:, t, :], stat[:, RDEN + t:RDEN + t + 1], None, ALU.mult)
                ins.then_inc(p_done, 1)

            def ptrans(h):
                for j in (1, 3):
                    dve.wait_ge(p_turned, 4 * h + j + 1)
                    dve.tensor_copy(probT[:, j, :], B[j][:, :]).then_inc(pt_dve, 1)

            def gla_cat(i):
                for c in (2 * i, 2 * i + 1):
                    dve.wait_ge(xhi_done, KT + c + 1)
                    dve.tensor_tensor(xT_lo[:, c, :], go[:, c, :], xT_hi[:, c, :].bitcast(F32), ALU.subtract)\
                        .then_inc(x_ready, 1)

            def attn_cat(_):
                dve.wait_ge(osum_done, GH + 1)
                inverse(B[1][:, :], rbc[:, :], AW, oinv_done)
                dve.wait_ge(orstd_done, GH + 1)
                for h in range(AH):
                    v = vcat[h % 2]
                    dve.scalar_tensor_tensor(out=v[:, :], in0=qT[h // 4][:, h % 4, :],
                                             scalar=par[:, G_AN + h:G_AN + h + 1], in1=rbc[:, :],
                                             op0=ALU.mult, op1=ALU.mult).then_inc(cat_v, 1)
                    dve.wait_ge(xhi_done, KT + AH + h + 1)
                    dve.tensor_tensor(xT_lo[:, AH + h, :], v[:, :], xT_hi[:, AH + h, :].bitcast(F32), ALU.subtract)\
                        .then_inc(x_ready, 1)
                    dve.wait_ge(x_ready, KT + AH + h + 1)

            pieces = {"gate": gate, "decay": decay, "keys": keys, "gla_out": gla_out, "gla_norm": gla_norm,
                      "states_a": lambda hd: states(hd, 0), "states_b": lambda hd: states(hd, 1),
                      "scores": scores, "pnorm": pnorm, "ptrans": ptrans, "gla_cat": gla_cat, "attn_cat": attn_cat}
            rotations = {START[name] + NSL - 1: (t, seq) for name, t, seq in
                         (("aq0", qT[0], 1 + 24), ("ak0", kT[0], 1 + 28), ("aq1", qT[1], 1 + 36), ("ak1", kT[1], 1 + 40))}

            for n in range(FF0):
                split(n + 2, n + 2)
                if n in rotations:
                    rotate(*rotations[n])
                for piece, arg in SIDE.get(n, ()):
                    if piece in pieces:
                        pieces[piece](arg)
                b, i = divmod(n - WG0, HALF)
                if n >= WG0 and i == HALF - 1:
                    j = b % 4
                    if b < 4:
                        dve.wait_ge(hid_in[j], 16)
                    for s in range(ST):
                        if s == 3:
                            dve.wait_ge(slab_done, n + 1)
                        else:
                            dve.wait_ge(bank_done, 3 * (len(IN_BLOCKS) + b) + s + 1)
                        h = hid[j][:, s, :]
                        if b >= 4:
                            dve.wait_ge(hid_added, 4 * (b - 4) + s + 1)
                        dve.tensor_tensor(h, h, A[s][:, :], ALU.add).then_inc(hid_added, 1)

            def row_norm(count, waited):
                dve.wait_ge(waited, count)
                ss = stat[:, SS2:SS2 + 16].rearrange("p (s j) -> p s j", j=4)
                link(dve.tensor_reduce(stat[:, RSTD:RSTD + ST], ss, AX_X, ALU.add))
                inverse(stat[:, RSTD:RSTD + ST], stat[:, RSTD:RSTD + ST], D, inv_done)

            row_norm(ST + 16, ssq_done)
            dve.wait_ge(rstd_done, 2)

            def scale_tile(k):
                if k >= 2:
                    dve.wait_ge(turned, KT + k - 1)
                j, c = divmod(k, 4)
                for s in range(ST):
                    ins = dve.tensor_scalar(hn[k % 2][:, s, :], hid[j][:, s, c * P:(c + 1) * P],
                                            stat[:, RSTD + s:RSTD + s + 1], None, ALU.mult)
                ins.then_inc(hn_done, 1)

            scale_tile(0)
            for k in range(KT):
                if k + 1 < KT:
                    scale_tile(k + 1)
                dve.wait_ge(xhi_done, 2 * KT + k + 1)
                dve.scalar_tensor_tensor(out=xT_lo[:, k, :], in0=B[k % 4][:, :],
                                         scalar=par[:, G_N2 + k:G_N2 + k + 1],
                                         in1=xT_hi[:, k, :].bitcast(F32), op0=ALU.mult, op1=ALU.subtract)\
                    .then_inc(x_ready, 1)

            def ffn(order, n0, g, step):
                for i, (what, k) in enumerate(order):
                    n = n0 + i + step * g
                    if what == "gate" and k == 0:
                        src = par[:, NROWS:].rearrange("p (q f) -> p q f", f=FT)[:, :, bass.ds(g * G, G)]
                        if step:
                            dve.wait_ge(conv2, G * g)
                        dve.tensor_copy(gpar[:, :, :], src).then_inc(gpar_done, 1)
                    if not (n0 + i >= LAST0 + len(LAST) - 2 and not step):
                        split(n0 + i + 2, n + 2)
                    if what == "gate" and k == NSL - 1:
                        dve.wait_ge(gpar_done, g + 1)
                        for m in range(4):
                            dve.wait_ge(conv1, G * g + m + 1)
                            dve.scalar_tensor_tensor(out=cv[:, m, 1:S], in0=A[m][:, 0:S - 1],
                                                     scalar=gpar[:, 0, m:m + 1], in1=cv[:, m, 1:S],
                                                     op0=ALU.mult, op1=ALU.add).then_inc(conv_first, 1)
                            dve.wait_ge(conv_first, G * g + m + 1)
                            dve.scalar_tensor_tensor(out=cv[:, m, 0:S - 1], in0=A[m][:, 1:S],
                                                     scalar=gpar[:, 2, m:m + 1], in1=cv[:, m, 0:S - 1],
                                                     op0=ALU.mult, op1=ALU.add).then_inc(conv2, 1)
                    if what == "up" and k == NSL - 1:
                        for m in range(4):
                            dve.wait_ge(silu_done, G * g + m + 1)
                            if m == 3:
                                dve.wait_ge(slab_done, n + 1)
                            else:
                                dve.wait_ge(bank_done, bank_base(what, 0, g, step) + m + 1)
                            dve.tensor_tensor(cv[:, m, :], cv[:, m, :], B[m][:, :], ALU.mult).then_inc(act_done, 1)
                        for m in range(4):
                            dve.wait_ge(ahi_done, G * g + m + 1)
                            dve.tensor_tensor(act_lo[:, m, :], cv[:, m, :], act_hi[:, m, :].bitcast(F32), ALU.subtract)\
                                .then_inc(alo_done, 1)
                    if what == "down" and k % 2:
                        j = k // 2
                        banks = B if j % 2 == 0 else A
                        for s in range(ST):
                            if s == 3:
                                dve.wait_ge(slab_done, n + 1)
                            elif step:
                                dve.wait_ge(bank_done, bank_base(what, j, g, step) + s + 1)
                            else:
                                dve.wait_ge(bank_done, bank_base("gate", 0, NG, 1) + 3 * j + s + 1)
                            h = hid[j][:, s, :]
                            dve.tensor_tensor(h, h, banks[s][:, :], ALU.add).then_inc(hid_added, 1)

            ffn(FIRST, FF0, 0, 0)
            with dve.Fori(1, NG) as g:
                ffn(ORDER, LOOP0 - GROUP, g, GROUP)
            ffn(LAST, LAST0, 0, 0)
            row_norm(16, fsq_done)
            dve.wait_ge(rstd_done, 3)
            dve.wait_ge(offs_in, 32)
            for j in range(4):
                for s in range(ST):
                    h = hid[j][:, s, :]
                    dve.scalar_tensor_tensor(out=h, in0=h, scalar=stat[:, RSTD + s:RSTD + s + 1],
                                             in1=gfin[:, j * BLK:(j + 1) * BLK], op0=ALU.mult, op1=ALU.mult)\
                        .then_inc(fin_done, 1)


_NAMES = ["x", "norm1_g", "w_in", "gf_up", "gf_b", "gb_up", "gb_b", "gla_norm_g", "attn_norm_g", "w_out",
          "norm2_g", "w_gate", "w_up", "conv_w", "conv_b", "w_down", "final_norm_g"]


def kernel(**inputs):
    import concourse.bacc as bacc
    from concourse.bass_utils import run_bass_kernel_spmd

    nc = bacc.Bacc("TRN2", target_bir_lowering=False, num_devices=1)
    arrays = {f"in_{k}": np.ascontiguousarray(inputs[k]) for k in _NAMES}
    arrays.update({f"in_{k}": np.ascontiguousarray(v) for k, v in
                   zip(("tables", "toep", "rope", "masks"), constant_tables())})
    aps = [nc.dram_tensor(k, a.shape, mybir.dt.from_np(a.dtype), kind="ExternalInput").ap() for k, a in arrays.items()]
    out = nc.dram_tensor("out", inputs["x"].shape, F32, kind="ExternalOutput").ap()
    encoder_block(nc, *aps, out)
    r = run_bass_kernel_spmd(nc, [arrays], core_ids=[0])
    return r.results[0]["out"]
```

```python
from contextlib import ExitStack

import concourse.bass as bass
import numpy as np
from concourse import mybir

F32 = mybir.dt.float32
F32R = mybir.dt.float32r
I32 = mybir.dt.int32
ALU = mybir.AluOpType
ACT = mybir.ActivationFunctionType
AX_X = mybir.AxisListType.X

P = 128
S = 512
D = 2048
ST = S // P
KT = D // P
EPS = 1e-6

AW = 1024
AH = 8
HD = AW // AH
ROPE = HD // 4
PATTERNS = ((128, 1), (512, 4), (2048, 16))
THETA = 500000.0
ASCALE = float(HD) ** -0.5

GH = 4
GK = 512
GV = 1024
DK = GK // GH
DV = GV // GH
RANK = 16
CH = 64
NC = S // CH
GSCALE = float(DK) ** -0.5

F = 5632
FT = F // P
G = 4
NG = FT // G

OFF_AQ, OFF_AK, OFF_AV = 0, AW, 2 * AW
OFF_GQ = 3 * AW
OFF_GK, OFF_GV = OFF_GQ + GK, OFF_GQ + 2 * GK
OFF_GR = OFF_GV + GV
OFF_Z = OFF_GR + GV
IN_W = OFF_Z + 2 * RANK

BLK = 512
KS = 2
SLAB = KS * BLK
NSL = KT // KS

IN_BLOCKS = [("gq", OFF_GQ, "f"), ("gk", OFF_GK, "f"), ("gr0", OFF_GR, "f"), ("gr1", OFF_GR + BLK, "f"),
             ("gv0", OFF_GV, "t"), ("gv1", OFF_GV + BLK, "t"),
             ("aq0", OFF_AQ, "f"), ("ak0", OFF_AK, "f"), ("av0", OFF_AV, "t"),
             ("aq1", OFF_AQ + BLK, "f"), ("ak1", OFF_AK + BLK, "f"), ("av1", OFF_AV + BLK, "t")]
Z_SLABS = 2
Z_COL = IN_W - P
Z_KS = KT // Z_SLABS
IN0 = Z_SLABS
WG0 = IN0 + NSL * len(IN_BLOCKS)
HALF = NSL // 2
WA0 = WG0 + HALF * (D // BLK)
FF0 = WA0 + HALF * (D // BLK)
GROUP = 2 * NSL + 2 * (D // BLK)
RING = 3

START = {name: IN0 + NSL * b for b, (name, _, _) in enumerate(IN_BLOCKS)}


def side_pieces():
    side = {}

    def put(n, piece, arg):
        side.setdefault(n, []).append((piece, arg))

    first = START["gv0"] + 4
    for hd in range(2 * GH):
        n = first + 4 * hd
        for k, piece in enumerate(("gate", "decay", "keys", "states_a", "states_b", "gla_out")):
            put(n + k, piece, hd)
        if hd % 2:
            put(n + 6, "gla_norm", hd // 2)
    for b in range(2):
        for i, name in enumerate((f"aq{b}", f"ak{b}")):
            for m in range(4):
                put(START[name] + NSL + m, "rotate", (b, i, m))
    for h in range(AH):
        n = START["aq1"] + 6 * h if h < 4 else WG0 + 3 * (h - 4)
        for k, piece in enumerate(("scores", "pnorm", "ptrans", "pv")):
            put(n + k, piece, h)
    for i in range(HALF):
        put(START["av1"] + i + 1, "gla_cat", i)
    for i in range(2):
        put(WG0 + 1 + i, "attn_cat", i)
    put(WA0 - 2, "attn_sum", 0)
    rank = {p: r for r, p in enumerate(("gla_norm", "gla_out", "gate", "states_a", "states_b", "keys", "decay", "pv"))}
    return {n: sorted(v, key=lambda x: rank.get(x[0], 99)) for n, v in side.items()}


SIDE = side_pieces()
NROWS = 2 * KT + AH + 2
G_N1, G_N2, G_AN, G_GN = 0, KT, 2 * KT, 2 * KT + AH
PCOLS = NROWS + 4 * FT
TAP = [NROWS + k * FT for k in range(3)]
CBIAS = NROWS + 3 * FT
TOEP = 2 * S - P
SCORE_ORDER = (1, 2, 3, 0)


def constant_tables():
    t = np.arange(P)
    same = (t[:, None] // CH) == (t[None, :] // CH)
    sums, masks = [], []
    for back in (False, True):
        seen = same & ((t[:, None] >= t[None, :]) if back else (t[:, None] <= t[None, :]))
        b = seen.astype(np.float64) / 16.0
        start = t // CH * CH
        ref = start + (CH // 2 if back else CH // 2 - 1)
        last = start + (0 if back else CH - 1)
        sums += [b - b[:, ref], b, b[:, last] - b]
        masks.append(seen.astype(np.int32))
    x = np.arange(TOEP)[None, :] - (S - P) - t[:, None]
    count = np.zeros(x.shape)
    for window, d in PATTERNS:
        count += (x % d == 0) & (np.abs(x) <= window // 2)
    toep = np.where(count > 0, np.log(np.maximum(count, 1)) / ASCALE, -1e30)
    floats = np.concatenate([np.eye(P)] + sums, axis=1).astype(np.float32)
    half = ROPE // 2
    ang = (np.float32(THETA) ** (-np.arange(0, ROPE, 2, dtype=np.float32) / np.float32(ROPE)))[:, None] \
        * np.arange(S, dtype=np.float32)[None, :]
    ang = ang.astype(np.float32).astype(np.float64)
    cos, sin = np.cos(ang), np.sin(ang)
    rope = np.concatenate([np.concatenate([cos, cos], 0), np.concatenate([-sin, sin], 0)], axis=1)
    assert rope.shape == (2 * half, 2 * S)
    return floats, toep.astype(np.float32), rope.astype(np.float32), np.concatenate(masks, axis=1)


def encoder_block(nc, x, norm1_g, w_in, gf_up, gf_b, gb_up, gb_b, gla_norm_g, attn_norm_g, w_out,
                  norm2_g, w_gate, w_up, conv_w, conv_b, w_down, final_norm_g, tables, toep, rope, masks, out):
    ctx = ExitStack()
    cursor = [(nc.sbuf_base + 31) // 32 * 32]

    def at(name, offset, shape, dt):
        return nc.alloc_sbuf_tensor_at(name, shape, dt, offset=offset)

    def sb(name, shape, dt=F32):
        size = int(np.prod(shape[1:])) * 4
        offset = cursor[0]
        cursor[0] += (size + 31) // 32 * 32
        return at(name, offset, shape, dt)

    with ctx:
        def sem(name):
            return ctx.enter_context(nc.semaphore(name))

        xT_hi = sb("xT_hi", [P, KT, S], F32R)
        xT_lo = sb("xT_lo", [P, KT, S], F32R)
        raw = [sb(f"raw{i}", [P, SLAB]) for i in range(RING)]
        w_hi = [sb(f"w_hi{i}", [P, SLAB], F32R) for i in range(RING)]
        w_lo = [sb(f"w_lo{i}", [P, SLAB], F32R) for i in range(RING)]
        tab = sb("tab", [P, 7 * P])
        ident = tab[:, 0:P]
        sums = [tab[:, P * (1 + i):P * (2 + i)] for i in range(6)]
        seen = sb("seen", [P, 2 * P], I32)
        ones = sb("ones", [P, P])
        small = sb("small", [P, 2 * S])
        zrope = sb("zrope", [P, S])
        par = sb("par", [P, PCOLS])
        stat = sb("stat", [P, 64])
        gpar = sb("gpar", [P, 4, G])
        KB = 1024
        arena = cursor[0]
        assert arena + 94 * KB <= nc.sbuf_top, (arena, nc.sbuf_top)

        def ar(name, kb, shape, dt=F32):
            return at(name, arena + int(kb * KB), shape, dt)

        xin = [ar(f"xin{s}", 8 * s, [P, D]) for s in range(ST)]
        junk = ar("junk", 64, [P, D])
        prow = ar("prow", 32, [P, 5, P])
        gq = ar("gq", 0, [P, GH, S])
        gk = ar("gk", 8, [P, GH, S])
        gv = ar("gv", 16, [P, ST, GV])
        go = ar("go", 32, [P, 2 * GH, S])
        qT = [ar("qT0", 48, [P, 4, S]), ar("qT1", 8, [P, 4, S])]
        kT = [ar("kT0", 56, [P, 4, S]), ar("kT1", 16, [P, 4, S])]
        vv = [ar("vv0", 0, [P, ST, BLK]), ar("vv1", 24, [P, ST, BLK])]
        e = [ar(f"e{i}", 64 + 2 * i, [P, S]) for i in range(4)]
        state = ar("state", 72, [P, NC, DV])
        osq = ar("osq", 72, [P, 2, S])
        kst = ar("kst", 80, [P, ST, P])
        at_m = [ar(f"at_m{i}", 82 + 2 * i, [P, ST, P]) for i in range(2)]
        gg = ar("gg", 86, [P, ST, P])
        gt = ar("gt", 88, [P, S])
        o_acc = ar("o_acc", 90, [P, 2, S])
        prob = ar("prob", 64, [P, ST, S])
        probT = ar("probT", 72, [P, ST, S])
        offs = ar("offs", 80, [P, TOEP])
        sq = [ar(f"sq{i}", 84 + 4 * i, [P, S]) for i in range(2)]
        sqsum = ar("sqsum", 86, [P, S])
        vcat = ar("vcat", 90, [P, 2, S])
        hid = [ar("hid0", 56, [P, ST, BLK]), ar("hid1", 0, [P, ST, BLK]),
               ar("hid2", 32, [P, ST, BLK]), ar("hid3", 40, [P, ST, BLK])]
        act_hi = ar("act_hi", 16, [P, G, S], F32R)
        act_lo = ar("act_lo", 24, [P, G, S], F32R)
        cv = ar("cv", 64, [P, G, S])
        hn = [ar(f"hn{i}", at_kb, [P, ST, P]) for i, at_kb in enumerate((72, 74, 86, 88))]
        sqj = ar("sqj", 76, [P, BLK])
        gfin = ar("gfin", 78, [P, D])

        acc = [ctx.enter_context(nc.psum_tensor(f"acc{i}", [P, BLK], F32)) for i in range(8)]
        A, B = acc[:4], acc[4:]

        SSQ, RSTD, SS2, MX, NMX, DEN, RDEN, DEC, ARSTD = 0, 4, 8, 24, 28, 32, 36, 40, 48

        tab_in = sem("tab_in")
        offs_in = sem("offs_in")
        x_in = [sem(f"x_in{s}") for s in range(ST)]
        w_in_sem = [sem(f"w_landed{i}") for i in range(RING)]
        hi_done = sem("hi_done")
        lo_done = sem("lo_done")
        slab_done = sem("slab_done")
        bank_done = sem("bank_done")
        hid_added = sem("hid_added")
        act_chain = sem("act_chain")
        dve_chain = sem("dve_chain")
        pool_init = sem("pool_init")
        pool_chain = sem("pool_chain")
        par_t = sem("par_t")
        par_done = sem("par_done")
        ssq_done = sem("ssq_done")
        inv_done = sem("inv_done")
        rstd_done = sem("rstd_done")
        xn_done = sem("xn_done")
        turned = sem("turned")
        xhi_done = sem("xhi_done")
        x_ready = sem("x_ready")
        gate_pre = sem("gate_pre")
        l_done = sem("l_done")
        g_done = sem("g_done")
        decay_done = sem("decay_done")
        exp_done = sem("exp_done")
        keys_done = sem("keys_done")
        kst_t = sem("kst_t")
        kst_done = sem("kst_done")
        at_done = sem("at_done")
        at_masked = sem("at_masked")
        kv_done = sem("kv_done")
        kv_used = sem("kv_used")
        o_done = sem("o_done")
        o_saved = sem("o_saved")
        osq_done = sem("osq_done")
        osum_done = sem("osum_done")
        oinv_done = sem("oinv_done")
        orstd_done = sem("orstd_done")
        go_done = sem("go_done")
        in_act = sem("in_act")
        rope_done = sem("rope_done")
        score_done = sem("score_done")
        max_done = sem("max_done")
        p_exp = sem("p_exp")
        p_done = sem("p_done")
        p_turned = sem("p_turned")
        pt_act = sem("pt_act")
        pt_dve = sem("pt_dve")
        pv_done = sem("pv_done")
        sq_done = sem("sq_done")
        asum_done = sem("asum_done")
        ainv_done = sem("ainv_done")
        arstd_done = sem("arstd_done")
        gain_in = sem("gain_in")
        gf_done = sem("gf_done")
        fin_act = sem("fin_act")
        sqsum_done = sem("sqsum_done")
        hid_in = [sem(f"hid_in{j}") for j in range(4)]
        hn_done = sem("hn_done")
        conv1 = sem("conv1")
        conv2 = sem("conv2")
        silu_done = sem("silu_done")
        act_done = sem("act_done")
        ahi_done = sem("ahi_done")
        alo_done = sem("alo_done")
        fsq_done = sem("fsq_done")
        fin_done = sem("fin_done")
        stored = sem("stored")
        gpar_done = sem("gpar_done")
        conv_first = sem("conv_first")

        w_in_t = w_in.rearrange("l (t p) n -> p (l t) n", p=P)
        w_out_t = w_out.rearrange("l (t p) n -> p (l t) n", p=P)
        w_gate_t = w_gate.rearrange("l (t p) n -> p (l t) n", p=P)
        w_up_t = w_up.rearrange("l (t p) n -> p (l t) n", p=P)
        w_down_t = w_down.rearrange("l (t p) n -> p (l t) n", p=P)
        x_t = x.rearrange("b (s p) n -> p (b s) n", p=P)
        out_t = out.rearrange("b (s p) n -> p (b s) n", p=P)

        def mixer_slab(n):
            if n < IN0:
                return w_in_t[:, Z_KS * n:Z_KS * (n + 1), Z_COL:Z_COL + P]
            if n < WG0:
                b, i = divmod(n - IN0, NSL)
                c = IN_BLOCKS[b][1]
                return w_in_t[:, KS * i:KS * (i + 1), c:c + BLK]
            b, i = divmod(n - WG0, HALF)
            t = KS * i + (KT // 2 if n < WA0 else 0)
            j = b % (D // BLK)
            return w_out_t[:, t:t + KS, j * BLK:(j + 1) * BLK]

        ORDER = [("gate", i) for i in range(NSL)] + [("down", i) for i in range(2 * (D // BLK))] \
            + [("up", i) for i in range(NSL)]
        FIRST = [w for w in ORDER if w[0] != "down"]
        LAST = [w for w in ORDER if w[0] == "down"]
        LOOP0 = FF0 + len(FIRST)
        LAST0 = LOOP0 + (NG - 1) * GROUP
        assert GROUP % RING == 0

        def ffn_slab(what, i, g):
            if what == "down":
                j, half = divmod(i, 2)
                src = w_down_t[:, bass.ds((g - 1) * G + half * KS, KS), j * BLK:(j + 1) * BLK]
                return src
            src = w_gate_t if what == "gate" else w_up_t
            return src[:, KS * i:KS * (i + 1), bass.ds(g * BLK, BLK)]

        def ksplit(t, n):
            return t.rearrange("p (k c) -> p k c", c=n)

        def bank_base(what, j, g, step):
            mixer = 3 * (len(IN_BLOCKS) + 2 * (D // BLK))
            per = 3 * (2 + D // BLK)
            if not step:
                return mixer + (0 if what == "gate" else 3)
            start = mixer + 6 + (g - 1) * per
            if what == "gate":
                return start
            if what == "down":
                return start + 3 + 3 * j
            return start + 3 + 3 * (D // BLK)

        block = ctx.enter_context(nc.Block())

        @block.sync
        def _(sp):
            def load(n0, src, g=0, step=0):
                slot = n0 % RING
                c = src.shape[2]
                if n0 >= RING or step:
                    sp.wait_ge(lo_done, n0 - RING + 1 + step * g)
                sp.dma_start(ksplit(raw[slot][:, :], c), src).then_inc(w_in_sem[slot], 16)

            for s in range(ST):
                sp.dma_start(xin[s][:, :], x_t[:, s, :]).then_inc(x_in[s], 16)
            for n in range(FF0):
                load(n, mixer_slab(n))
            for i, (what, k) in enumerate(FIRST):
                load(FF0 + i, ffn_slab(what, k, 0))
            with sp.Fori(1, NG) as g:
                for i, (what, k) in enumerate(ORDER):
                    load(LOOP0 - GROUP + i, ffn_slab(what, k, g), g, GROUP)
            for i, (what, k) in enumerate(LAST):
                load(LAST0 + i, ffn_slab(what, k, NG))
            for q in range(2):
                for done, j in ((fin_act, 0), (fin_done, 2)):
                    for half in range(2):
                        sp.wait_ge(done, 4 * q + 2 * half + 2)
                        t = slice(2 * half, 2 * half + 2)
                        sp.dma_start(out_t[:, t, (j + q) * BLK:(j + q + 1) * BLK], hid[j + q][:, t, :])\
                            .then_inc(stored, 16)
            sp.wait_ge(stored, 16 * 8)

        @block.gpsimd
        def _(pool):
            for n, (view, value) in enumerate(((ones[:, :], 1.0), (small[64:96, :], 0.0), (zrope[64:96, :], 0.0),
                                               (zrope[64:65, :], 1.0), (small[96:128, :], 0.0))):
                pool.memset(view, value).then_inc(pool_init, 1)
                pool.wait_ge(pool_init, n + 1)
            pool.dma_start(tab[:, P:], tables[:, P:]).then_inc(tab_in, 16)
            pool.dma_start(seen[:, :], masks).then_inc(tab_in, 16)
            pool.dma_start(small[0:ROPE, :], rope).then_inc(tab_in, 16)
            for d, (up, bias) in enumerate(((gf_up, gf_b), (gb_up, gb_b))):
                pool.dma_start(small[64:65, d * GK:(d + 1) * GK], bias).then_inc(tab_in, 16)
                pool.dma_start(small[96 + RANK * d:96 + RANK * (d + 1), d * GK:(d + 1) * GK], up[0])\
                    .then_inc(tab_in, 16)
            for k in range(3):
                pool.dma_start(prow[0:FT, 1 + k, :], conv_w[0, k, :].rearrange("(r c) -> r c", c=P))\
                    .then_inc(tab_in, 16)
            pool.dma_start(prow[0:FT, 4, :], conv_b.rearrange("l (r c) -> (l r) c", c=P)).then_inc(tab_in, 16)

            pool.wait_ge(xn_done, ST)
            for i in range(2):
                pool.memset(at_m[i][:, :, :], 0.0).then_inc(pool_init, 1)
                pool.wait_ge(pool_init, 6 + i)
            pool.wait_ge(go_done, GH)
            pool.dma_start(offs[:, :], toep).then_inc(offs_in, 16)
            for h in range(AH):
                pool.wait_ge(sq_done, h + 1)
                if h == 0:
                    pool.tensor_copy(sqsum[:, :], sq[0][:, :]).then_inc(sqsum_done, 1)
                else:
                    pool.wait_ge(sqsum_done, h)
                    pool.tensor_tensor(sqsum[:, :], sqsum[:, :], sq[h % 2][:, :], ALU.add).then_inc(sqsum_done, 1)
                if h == 3:
                    pool.wait_ge(x_ready, KT + 2 * GH)
                    for j in range(4):
                        pool.dma_start(hid[j][:, :, :], x_t[:, :, j * BLK:(j + 1) * BLK]).then_inc(hid_in[j], 16)
            pool.wait_ge(x_ready, 3 * KT)
            pool.dma_start(gfin[:, :], final_norm_g.partition_broadcast(P)).then_inc(offs_in, 16)
            pool.wait_ge(offs_in, 32)
            for j in range(3):
                for s in range(ST):
                    pool.wait_ge(fsq_done, 4 * j + s + 1)
                    h = hid[j][:, s, :]
                    pool.tensor_tensor(h, h, gfin[:, j * BLK:(j + 1) * BLK], ALU.mult).then_inc(gf_done, 1)
                    pool.wait_ge(gf_done, 4 * j + s + 1)

        n_tab = 16 * (3 + 4 + 4)

        IN_BANKS = 1 + 4 * len(IN_BLOCKS)
        OUT_BANKS = 4 * 2 * (D // BLK)
        DOWN_BANKS = 4 * (D // BLK)

        @block.tensor
        def _(pe):
            def three(o, wh, wl, ah, al, first, last, weights_first):
                for k, (w, a) in enumerate(((wh, ah), (wh, al), (wl, ah))):
                    lhs, rhs = (w, a) if weights_first else (a, w)
                    mm = pe.matmul(o, lhs, rhs, start=first and k == 0, stop=last and k == 2)
                return mm

            def slab(n0, wait, kind, banks, k0, first, last, free=None, inputs=(xT_hi, xT_lo)):
                slot = n0 % RING
                pe.wait_ge(lo_done, wait + 1)
                hi, lo = ksplit(w_hi[slot][:, :], BLK), ksplit(w_lo[slot][:, :], BLK)
                for m in range(4):
                    if first:
                        free(m)
                    c = slice(m * P, (m + 1) * P)
                    for k in range(KS):
                        a, al = inputs[0][:, k0 + k], inputs[1][:, k0 + k]
                        if kind == "f":
                            wh, wl = hi[:, k, c], lo[:, k, c]
                        else:
                            wh, wl, a, al = hi[:, k, :], lo[:, k, :], a[:, c], al[:, c]
                        mm = three(banks[m][:, :], wh, wl, a, al, first and k == 0, last and k == KS - 1, kind == "f")
                    if m == 3:
                        mm.then_inc(slab_done, 1)
                    elif last:
                        mm.then_inc(bank_done, 1)

            def turn_rows(k):
                r, c = (NROWS, 0) if k == 0 else (FT, NROWS + (k - 1) * FT)
                return pe.transpose(B[0][:, c:c + r], prow[0:r, k, :], ident[0:r, 0:r])

            pe.wait_ge(gain_in, 16 * 5)
            turn_rows(0).then_inc(par_t, 1)

            def turn_tile(k, src, seq):
                if seq >= 4:
                    pe.wait_ge(x_ready, seq - 3)
                for s in range(ST):
                    mm = pe.transpose(B[k % 4][:, s * P:(s + 1) * P], src(s), ident)
                mm.then_inc(turned, 1)

            pe.wait_ge(xn_done, ST)
            pe.wait_ge(par_done, 1)

            def turn_x(k):
                turn_tile(k, lambda s: xin[s][:, k * P:(k + 1) * P], k)

            for k in range(4):
                turn_x(k)

            def gate(hd):
                h, d = divmod(hd, 2)
                if hd == 0:
                    pe.wait_ge(in_act, 1)
                    pe.wait_ge(par_done, 2)
                w = small[64:P, d * GK + h * DK:d * GK + (h + 1) * DK]
                for t in range(ST):
                    mm = pe.matmul(B[0][:, t * P:(t + 1) * P], zrope[64:P, t * P:(t + 1) * P], w, start=True, stop=True)
                mm.then_inc(gate_pre, 1)

            def decay(hd):
                d = hd % 2
                pe.wait_ge(g_done, hd + 1)
                if hd:
                    pe.wait_ge(kv_used, 2 * hd)
                for i, b in ((1, 2), (2, 3), (0, 1)):
                    if hd and b == 1:
                        pe.wait_ge(o_saved, hd)
                    for t in range(ST):
                        mm = pe.matmul(B[b][:, t * P:(t + 1) * P], gg[:, t, :], sums[3 * d + i], start=True, stop=True)
                mm.then_inc(decay_done, 1)

            def keys(hd):
                pe.wait_ge(keys_done, hd + 1)
                for t in range(ST):
                    mm = pe.transpose(B[0][:, t * P:(t + 1) * P], e[3][:, t * P:(t + 1) * P], ident)
                mm.then_inc(kst_t, 1)
                for t in range(ST):
                    c = slice(t * P, (t + 1) * P)
                    mm = pe.matmul(B[1][:, c], e[1][:, c], e[0][:, c], start=True, stop=True)
                mm.then_inc(at_done, 1)

            def states(hd, part):
                h, d = divmod(hd, 2)
                if part == 0:
                    pe.wait_ge(kst_done, hd + 1)
                    pe.wait_ge(in_act, 1 + 4 * (5 + h // 2))
                    if d == 0 and h:
                        pe.wait_ge(oinv_done, h)
                else:
                    pe.wait_ge(kv_used, 2 * hd + 1)
                for i in range(4 - part):
                    step = 4 * part + i
                    c = NC - 1 - step if d else step
                    r = (c % 2) * CH
                    o = B[2 + c % 2][:, (i // 2) * DV:(i // 2 + 1) * DV]
                    mm = pe.matmul(o, kst[r:r + CH, c // 2, :], gv[r:r + CH, c // 2, h * DV:(h + 1) * DV],
                                   start=True, stop=True)
                mm.then_inc(kv_done, 1)

            def gla_out(hd):
                h, d = divmod(hd, 2)
                pe.wait_ge(at_masked, hd + 1)
                pe.wait_ge(kv_used, 2 * hd + 2)
                if hd + 1 < 2 * GH:
                    pe.wait_ge(g_done, hd + 2)
                for v in range(2):
                    for t in range(ST):
                        c = slice(t * P, (t + 1) * P)
                        pe.matmul(B[v][:, c], gv[:, t, h * DV + v * P:h * DV + (v + 1) * P],
                                  at_m[d][:, t, :], start=(t == 0), stop=False, skip_group_check=True)
                    for c in range(NC - 1):
                        c = c if d else c + 1
                        mm = pe.matmul(B[v][:, c * CH:(c + 1) * CH], state[:, c, v * P:(v + 1) * P],
                                       e[2][:, c * CH:(c + 1) * CH], start=False, stop=True, skip_group_check=True)
                mm.then_inc(o_done, 1)

            def gla_norm(h):
                pe.wait_ge(osq_done, h + 1)
                nxt = 2 * h + 2
                if nxt < 2 * GH:
                    pe.wait_ge(exp_done, nxt + 1)
                for v in range(2):
                    mm = pe.matmul(B[3][:, :], ones[:, :], osq[:, v, :], start=(v == 0), stop=(v == 1))
                mm.then_inc(osum_done, 1)

            def scores(h):
                b, hh = divmod(h, 4)
                pe.wait_ge(rope_done, 8 * b + 4 + hh + 1)
                if h == 0:
                    pe.wait_ge(oinv_done, GH)
                    pe.wait_ge(o_saved, 2 * GH)
                else:
                    pe.wait_ge(pt_act, 2 * h)
                    pe.wait_ge(pt_dve, 2 * h)
                for t in SCORE_ORDER:
                    if h and t == 0:
                        pe.wait_ge(sq_done, h)
                        if h > 4:
                            pe.wait_ge(x_ready, KT + 2 * GH + h)
                    pe.matmul(B[t][:, :], qT[b][:, hh, t * P:(t + 1) * P], kT[b][:, hh, :], start=True, stop=True)\
                        .then_inc(score_done, 1)

            def ptrans(h):
                pe.wait_ge(p_done, h + 1)
                for j in range(ST):
                    for t in range(ST):
                        mm = pe.transpose(B[j][:, t * P:(t + 1) * P], prob[:, t, j * P:(j + 1) * P], ident)
                    mm.then_inc(p_turned, 1)

            def pv(h):
                b, hh = divmod(h, 4)
                pe.wait_ge(pt_act, 2 * h + 2)
                pe.wait_ge(pt_dve, 2 * h + 2)
                if hh == 0:
                    pe.wait_ge(in_act, 1 + 4 * (9 if b == 0 else 12))
                for j in range(ST):
                    mm = pe.matmul(B[0][:, :], vv[b][:, j, hh * HD:(hh + 1) * HD], probT[:, j, :],
                                   start=(j == 0), stop=(j == ST - 1))
                mm.then_inc(pv_done, 1)

            def attn_sum(_):
                pe.wait_ge(sqsum_done, AH)
                pe.wait_ge(pt_dve, 2 * AH)
                for t in range(ST):
                    mm = pe.matmul(B[1][:, t:t + 1], sqsum[:, t * P:(t + 1) * P], ones[:, 0:1], start=True, stop=True)
                mm.then_inc(asum_done, 1)

            pieces = {"gate": gate, "decay": decay, "keys": keys, "gla_out": gla_out, "gla_norm": gla_norm,
                      "states_a": lambda hd: states(hd, 0), "states_b": lambda hd: states(hd, 1),
                      "scores": scores, "ptrans": ptrans, "pv": pv, "attn_sum": attn_sum}

            for n in range(FF0):
                if n < IN0:
                    pe.wait_ge(lo_done, n + 1)
                    hi, lo = ksplit(w_hi[n][:, :], P), ksplit(w_lo[n][:, :], P)
                    for k in range(Z_KS):
                        kk = Z_KS * n + k
                        pe.wait_ge(x_ready, kk + 1)
                        if kk + 4 < KT:
                            turn_x(kk + 4)
                        mm = three(A[0][:, :], hi[:, k, :], lo[:, k, :], xT_hi[:, kk, :], xT_lo[:, kk, :],
                                   kk == 0, kk == KT - 1, True)
                    mm.then_inc(slab_done, 1)
                elif n < WG0:
                    b, i = divmod(n - IN0, NSL)
                    if n == IN0 + 2:
                        pe.wait_ge(tab_in, n_tab)
                        for k in range(1, 5):
                            mm = turn_rows(k)
                        mm.then_inc(par_t, 1)

                    def in_free(m):
                        pe.wait_ge(in_act, 1 + 4 * (b - 1) + m + 1 if b else 1)

                    slab(n, n, IN_BLOCKS[b][2], A, KS * i, i == 0, i == NSL - 1, in_free)
                else:
                    b, i = divmod(n - WG0, HALF)
                    k0 = KS * i + (0 if n < WA0 else KT // 2)
                    pe.wait_ge(x_ready, KT + k0 + KS)

                    def out_free(m):
                        if b == 0:
                            pe.wait_ge(in_act, IN_BANKS - 3 + m)
                        else:
                            pe.wait_ge(hid_added, 4 * (b - 1) + m + 1)

                    slab(n, n, "t", A, k0, i == 0, i == HALF - 1, out_free)
                for piece, arg in SIDE.get(n, ()):
                    if piece in pieces:
                        pieces[piece](arg)

            def turn_h(k):
                pe.wait_ge(hn_done, k + 1)
                turn_tile(k, lambda s: hn[k % 4][:, s, :], 2 * KT + k)

            for k in range(4):
                turn_h(k)

            def ffn(order, n0, g, step, opening):
                added = OUT_BANKS + DOWN_BANKS * (g - 1)
                for i, (what, k) in enumerate(order):
                    n = n0 + i + step * g
                    if what == "down":
                        j, half = divmod(k, 2)
                        if k == 0:
                            pe.wait_ge(alo_done, G * g)

                        def free(m):
                            if j == 0:
                                pe.wait_ge(act_done, G * (g - 1) + m + 1)
                            elif j == 1 and opening == "last":
                                pe.wait_ge(hid_added, added - 4 + m + 1)
                            elif j == 1:
                                pe.wait_ge(conv2, G * g + m + 1)
                            else:
                                pe.wait_ge(hid_added, added + 4 * (j - 2) + m + 1)

                        slab(n0 + i, n, "t", B if j % 2 == 0 else A, half * KS, half == 0, half == 1, free,
                             (act_hi, act_lo))
                    elif what == "gate":
                        if opening == "first":
                            pe.wait_ge(x_ready, 2 * KT + KS * (k + 1))
                            for t in range(4 + KS * k, min(4 + KS * (k + 1), KT)):
                                turn_h(t)

                        def free(m):
                            if opening == "first":
                                pe.wait_ge(hid_added, OUT_BANKS - 4 + m + 1)
                            else:
                                pe.wait_ge(conv2, G * (g - 1) + m + 1)
                                pe.wait_ge(hid_added, added - 4 + m + 1)

                        slab(n0 + i, n, "f", A, KS * k, k == 0, k == NSL - 1, free)
                    else:
                        def free(m):
                            if opening == "first":
                                pe.wait_ge(x_ready, 3 * KT)
                            else:
                                pe.wait_ge(hid_added, added + 8 + m + 1)

                        slab(n0 + i, n, "f", B, KS * k, k == 0, k == NSL - 1, free)

            ffn(FIRST, FF0, 0, 0, "first")
            with pe.Fori(1, NG) as g:
                ffn(ORDER, LOOP0 - GROUP, g, GROUP, "loop")
            ffn(LAST, LAST0, NG, 0, "last")

        @block.scalar
        def _(act):
            chain = [0]

            def link(ins):
                chain[0] += 1
                ins.then_inc(act_chain, 1)
                act.wait_ge(act_chain, chain[0])

            def split(n0, wait, g8):
                slot = n0 % RING
                act.wait_ge(w_in_sem[slot], 16 * (n0 // RING + 1) + 16 * g8)
                if n0 >= RING:
                    act.wait_ge(slab_done, wait - RING + 1)
                act.activation(w_hi[slot][:, :], raw[slot][:, :], ACT.Copy).then_inc(hi_done, 1)

            act.dma_start(ident, tables[:, 0:P]).then_inc(gain_in, 16)
            for src, r in ((norm1_g, G_N1), (norm2_g, G_N2), (attn_norm_g, G_AN), (gla_norm_g, G_GN)):
                k = src.shape[1] // P
                act.dma_start(prow[r:r + k, 0, :], src.rearrange("l (r c) -> (l r) c", c=P)).then_inc(gain_in, 16)
            act.wait_ge(par_t, 1)
            act.activation(par[:, 0:NROWS], B[0][:, 0:NROWS], ACT.Copy).then_inc(par_done, 1)
            for s in range(ST):
                act.wait_ge(x_in[s], 16)
                if s:
                    act.wait_ge(ssq_done, s)
                act.activation(junk[:, :], xin[s][:, :], ACT.Square, accum_out=stat[:, SSQ + s:SSQ + s + 1])\
                    .then_inc(ssq_done, 1)
            act.wait_ge(inv_done, 1)
            act.activation(stat[:, RSTD:RSTD + ST], stat[:, RSTD:RSTD + ST], ACT.Sqrt).then_inc(rstd_done, 1)
            act.wait_ge(par_done, 1)
            split(0, 0, 0)
            split(1, 1, 0)

            def tile_hi(k, g0, seq):
                act.wait_ge(turned, seq + 1)
                act.activation(xT_hi[:, k, :], B[k % 4][:, :], ACT.Copy, scale=par[:, g0 + k:g0 + k + 1])\
                    .then_inc(xhi_done, 1)

            for k in range(KT):
                tile_hi(k, G_N1, k)
                if k == KT // 2:
                    split(2, 2, 0)

            def evac_in(n):
                if n == IN0 - 1:
                    act.wait_ge(slab_done, IN0)
                    act.activation(zrope[96:P, :], A[0][96:P, :], ACT.Copy).then_inc(in_act, 1)
                    return
                b, i = divmod(n - IN0, NSL)
                if n < IN0 or n >= WG0 or i != NSL - 1:
                    return
                name = IN_BLOCKS[b][0]
                if name in ("av0", "aq1", "ak1", "av1"):
                    act.wait_ge(go_done, GH)
                for m in range(4):
                    if m == 3:
                        act.wait_ge(slab_done, n + 1)
                    else:
                        act.wait_ge(bank_done, 3 * b + m + 1)
                    src, fn, scale = A[m][:, :], ACT.Copy, 1.0
                    if name == "gq":
                        dst, scale = gq[:, m, :], GSCALE
                    elif name == "gk":
                        dst = gk[:, m, :]
                    elif name[:2] == "gr":
                        dst, fn = go[:, 4 * int(name[2]) + m, :], ACT.Silu
                    elif name[:2] == "gv":
                        v = int(name[2])
                        dst = gv[:, m, v * BLK:(v + 1) * BLK]
                    elif name[:2] == "aq":
                        dst = qT[int(name[2])][:, m, :]
                    elif name[:2] == "ak":
                        dst = kT[int(name[2])][:, m, :]
                    else:
                        dst = vv[int(name[2])][:, m, :]
                    act.activation(dst, src, fn, scale=scale).then_inc(in_act, 1)

            def gate(hd):
                act.wait_ge(gate_pre, hd + 1)
                if hd:
                    act.wait_ge(g_done, hd)
                if hd >= 3:
                    act.wait_ge(go_done, (hd - 1) // 2)
                link(act.activation(gt[:, :], B[0][:, :], ACT.Abs))
                link(act.activation(gt[:, :], gt[:, :], ACT.Exp, scale=-1.0))
                act.activation(gt[:, :], gt[:, :], ACT.Ln, bias=1.0).then_inc(l_done, 1)

            def decay(hd):
                act.wait_ge(decay_done, hd + 1)
                if hd:
                    act.wait_ge(o_done, hd)
                d = hd % 2
                act.activation(e[0][:, :], B[1][:, :], ACT.Exp)
                act.activation(e[1][:, :], B[1][:, :], ACT.Exp, scale=-1.0)
                act.activation(e[2][:, :], B[2][:, :], ACT.Exp)
                last = B[2][:, :].rearrange("p (c t) -> p c t", t=CH)[:, :, 0 if d else CH - 1]
                act.activation(stat[:, DEC:DEC + NC], last, ACT.Exp)
                act.activation(e[3][:, :], B[3][:, :], ACT.Exp).then_inc(exp_done, 1)

            def keys(hd):
                act.wait_ge(kst_t, hd + 1)
                act.activation(kst[:, :, :], B[0][:, :].rearrange("p (t k) -> p t k", k=P), ACT.Copy)\
                    .then_inc(kst_done, 1)

            def gla_out(hd):
                if hd % 2:
                    h = hd // 2
                    act.wait_ge(o_saved, hd + 1)
                    for v in range(2):
                        ins = act.activation(osq[:, v, :], o_acc[:, v, :], ACT.Square)
                    ins.then_inc(osq_done, 1)

            def gla_norm(h):
                act.wait_ge(oinv_done, h + 1)
                act.activation(gt[:, :], gt[:, :], ACT.Sqrt).then_inc(orstd_done, 1)

            def scores(h):
                act.wait_ge(max_done, h + 1)
                for t in range(ST):
                    ins = act.activation(prob[:, t, :], prob[:, t, :], ACT.Exp, bias=stat[:, NMX + t:NMX + t + 1],
                                         accum_out=stat[:, DEN + t:DEN + t + 1])
                ins.then_inc(p_exp, 1)

            def ptrans(h):
                for j in (0, 2):
                    act.wait_ge(p_turned, 4 * h + j + 1)
                    act.activation(probT[:, j, :], B[j][:, :], ACT.Copy).then_inc(pt_act, 1)

            def pv(h):
                act.wait_ge(pv_done, h + 1)
                if h < 4:
                    act.activation(qT[0][:, h, :], B[0][:, :], ACT.Copy)
                else:
                    act.activation(xT_hi[:, AH + h, :], B[0][:, :], ACT.Copy, scale=par[:, G_AN + h:G_AN + h + 1])\
                        .then_inc(xhi_done, 1)
                if h >= 2:
                    act.wait_ge(sqsum_done, h - 1)
                act.activation(sq[h % 2][:, :], B[0][:, :], ACT.Square).then_inc(sq_done, 1)

            def gla_cat(i):
                act.wait_ge(slab_done, START["av1"] + i + 1)
                for c in (2 * i, 2 * i + 1):
                    act.activation(xT_hi[:, c, :], go[:, c, :], ACT.Copy).then_inc(xhi_done, 1)

            def attn_cat(i):
                act.wait_ge(slab_done, WG0)
                for h in (2 * i, 2 * i + 1):
                    act.activation(xT_hi[:, AH + h, :], qT[0][:, h, :], ACT.Copy, scale=par[:, G_AN + h:G_AN + h + 1])\
                        .then_inc(xhi_done, 1)

            def attn_sum(_):
                act.wait_ge(ainv_done, 1)
                act.activation(stat[:, ARSTD:ARSTD + ST], stat[:, ARSTD:ARSTD + ST], ACT.Sqrt).then_inc(arstd_done, 1)

            pieces = {"gate": gate, "decay": decay, "keys": keys, "gla_out": gla_out, "gla_norm": gla_norm,
                      "scores": scores, "ptrans": ptrans, "pv": pv, "gla_cat": gla_cat, "attn_cat": attn_cat,
                      "attn_sum": attn_sum}
            for n in range(FF0):
                if n:
                    split(n + 2, n + 2, 0)
                if n == IN0 + 2:
                    act.wait_ge(par_t, 2)
                    act.activation(par[:, NROWS:], B[0][:, NROWS:PCOLS], ACT.Copy).then_inc(par_done, 1)
                evac_in(n)
                for piece, arg in SIDE.get(n, ()):
                    if piece in pieces:
                        pieces[piece](arg)
                if n >= WA0 and (n - WA0) % HALF == HALF - 1:
                    j = (n - WA0) // HALF
                    for s in range(ST):
                        act.wait_ge(hid_added, OUT_BANKS // 2 + 4 * j + s + 1)
                        act.activation(sqj[:, :], hid[j][:, s, :], ACT.Square,
                                       accum_out=stat[:, SS2 + 4 * s + j:SS2 + 4 * s + j + 1]).then_inc(ssq_done, 1)
                        act.wait_ge(ssq_done, ST + 4 * j + s + 1)
            act.wait_ge(inv_done, 2)
            act.activation(stat[:, RSTD:RSTD + ST], stat[:, RSTD:RSTD + ST], ACT.Sqrt).then_inc(rstd_done, 1)
            for k in range(4):
                tile_hi(k, G_N2, KT + k)

            def ffn(order, n0, g, step):
                for i, (what, k) in enumerate(order):
                    n = n0 + i + step * g
                    if not (n0 + i >= LAST0 + len(LAST) - 2 and not step):
                        split(n0 + i + 2, n + 2, (step // RING) * g)
                    if order is FIRST and what == "gate":
                        for t in range(4 + KS * k, min(4 + KS * (k + 1), KT)):
                            tile_hi(t, G_N2, KT + t)
                    if what == "gate" and k == NSL - 1:
                        for m in range(4):
                            act.wait_ge(gpar_done, g + 1)
                            if m == 3:
                                act.wait_ge(slab_done, n + 1)
                            else:
                                act.wait_ge(bank_done, bank_base(what, 0, g, step) + m + 1)
                            if step:
                                act.wait_ge(alo_done, G * g - G + m + 1)
                            act.activation(cv[:, m, :], A[m][:, :], ACT.Identity, bias=gpar[:, 3, m:m + 1],
                                           scale=gpar[:, 1, m:m + 1]).then_inc(conv1, 1)
                        for m in range(4):
                            act.wait_ge(conv2, G * g + m + 1)
                            act.activation(cv[:, m, :], cv[:, m, :], ACT.Silu).then_inc(silu_done, 1)
                    if what == "up" and k == NSL - 1:
                        for m in range(4):
                            act.wait_ge(act_done, G * g + m + 1)
                            act.activation(act_hi[:, m, :], cv[:, m, :], ACT.Copy).then_inc(ahi_done, 1)

            ffn(FIRST, FF0, 0, 0)
            with act.Fori(1, NG) as g:
                ffn(ORDER, LOOP0 - GROUP, g, GROUP)
            ffn(LAST, LAST0, 0, 0)
            for j in range(4):
                for s in range(ST):
                    act.wait_ge(hid_added, OUT_BANKS + DOWN_BANKS * (NG - 1) + 4 * j + s + 1)
                    act.activation(sqj[:, :], hid[j][:, s, :], ACT.Square,
                                   accum_out=stat[:, SS2 + 4 * s + j:SS2 + 4 * s + j + 1]).then_inc(fsq_done, 1)
                    act.wait_ge(fsq_done, 4 * j + s + 1)
            act.wait_ge(inv_done, 3)
            act.activation(stat[:, RSTD:RSTD + ST], stat[:, RSTD:RSTD + ST], ACT.Sqrt).then_inc(rstd_done, 1)
            act.wait_ge(rstd_done, 3)
            for j in range(2):
                for s in range(ST):
                    act.wait_ge(gf_done, 4 * j + s + 1)
                    act.activation(hid[j][:, s, :], hid[j][:, s, :], ACT.Copy, scale=stat[:, RSTD + s:RSTD + s + 1])\
                        .then_inc(fin_act, 1)

        @block.vector
        def _(dve):
            chain = [0]

            def link(ins):
                chain[0] += 1
                ins.then_inc(dve_chain, 1)
                dve.wait_ge(dve_chain, chain[0])

            def split(n0, wait):
                slot = n0 % RING
                dve.wait_ge(hi_done, wait + 1)
                dve.tensor_tensor(w_lo[slot][:, :], raw[slot][:, :], w_hi[slot][:, :].bitcast(F32), ALU.subtract)\
                    .then_inc(lo_done, 1)

            def inverse(src, dst, width, waited):
                link(dve.tensor_scalar(dst, src, 1.0 / width, EPS, ALU.mult, ALU.add))
                dve.reciprocal(dst, dst).then_inc(waited, 1)

            dve.wait_ge(ssq_done, ST)
            inverse(stat[:, SSQ:SSQ + ST], stat[:, RSTD:RSTD + ST], D, inv_done)
            dve.wait_ge(rstd_done, 1)
            for s in range(ST):
                dve.tensor_scalar(xin[s][:, :], xin[s][:, :], stat[:, RSTD + s:RSTD + s + 1], None, ALU.mult)\
                    .then_inc(xn_done, 1)

            def tile_lo(k, g0, seq):
                dve.wait_ge(xhi_done, seq + 1)
                dve.scalar_tensor_tensor(out=xT_lo[:, k, :], in0=B[k % 4][:, :], scalar=par[:, g0 + k:g0 + k + 1],
                                         in1=xT_hi[:, k, :].bitcast(F32), op0=ALU.mult, op1=ALU.subtract)\
                    .then_inc(x_ready, 1)

            split(0, 0)
            split(1, 1)
            dve.wait_ge(par_done, 1)
            for k in range(KT):
                tile_lo(k, G_N1, k)
                if k == KT // 2:
                    split(2, 2)

            swap = [(r + ROPE // 2) % ROPE for r in range(ROPE)]

            def rotate(arg):
                b, i, m = arg
                dve.wait_ge(in_act, 1 + 4 * (6 + 3 * b + i) + m + 1)
                src = (qT, kT)[i][b][0:ROPE, m, :]
                if rotated:
                    dve.wait_ge(rope_done, len(rotated))
                rotated.append(arg)
                link(dve.stream_shuffle(zrope[0:ROPE, :], src, swap))
                dve.tensor_tensor(zrope[0:ROPE, :], zrope[0:ROPE, :], small[0:ROPE, S:2 * S], ALU.mult)
                link(dve.tensor_tensor(src, src, small[0:ROPE, 0:S], ALU.mult))
                dve.tensor_tensor(src, src, zrope[0:ROPE, :], ALU.add).then_inc(rope_done, 1)

            rotated = []

            def gate(hd):
                dve.wait_ge(l_done, hd + 1)
                if hd:
                    dve.wait_ge(decay_done, hd)
                dve.scalar_tensor_tensor(out=gg[:, :, :].rearrange("p t k -> p (t k)"), in0=B[0][:, :], scalar=0.0,
                                         in1=gt[:, :], op0=ALU.min, op1=ALU.subtract).then_inc(g_done, 1)

            def decay(hd):
                h = hd // 2
                dve.wait_ge(exp_done, hd + 1)
                dve.wait_ge(in_act, 1 + 8)
                for i, src in enumerate((gq, gk, gq, gk)):
                    ins = dve.tensor_tensor(e[i][:, :], e[i][:, :], src[:, h, :], ALU.mult)
                ins.then_inc(keys_done, 1)

            def keys(hd):
                d = hd % 2
                dve.wait_ge(at_done, hd + 1)
                if hd == 0:
                    dve.wait_ge(pool_init, 7)
                mask = seen[:, d * P:(d + 1) * P]
                for t in range(ST):
                    ins = dve.copy_predicated(at_m[d][:, t, :], mask, B[1][:, t * P:(t + 1) * P])
                ins.then_inc(at_masked, 1)

            def states(hd, part):
                d = hd % 2
                dve.wait_ge(kv_done, 2 * hd + part + 1)
                for i in range(4):
                    step = 4 * part + i
                    c = NC - 1 - step if d else step
                    nxt = c - 1 if d else c + 1
                    kv = B[2 + c % 2][:, (i // 2) * DV:(i // 2 + 1) * DV]
                    if step == 0:
                        link(dve.tensor_copy(state[:, nxt, :], kv))
                    elif step < NC - 1:
                        ins = dve.scalar_tensor_tensor(out=state[:, nxt, :], in0=state[:, c, :],
                                                       scalar=stat[:, DEC + c:DEC + c + 1], in1=kv,
                                                       op0=ALU.mult, op1=ALU.add)
                        if i == 3 or step == NC - 2:
                            ins.then_inc(kv_used, 1)
                            dve.wait_ge(kv_used, 2 * hd + part + 1)
                        else:
                            link(ins)

            def gla_out(hd):
                d = hd % 2
                dve.wait_ge(o_done, hd + 1)
                for v in range(2):
                    if d == 0:
                        ins = dve.tensor_copy(o_acc[:, v, :], B[v][:, :])
                    else:
                        ins = dve.tensor_tensor(o_acc[:, v, :], o_acc[:, v, :], B[v][:, :], ALU.add)
                ins.then_inc(o_saved, 1)

            def gla_norm(h):
                dve.wait_ge(osum_done, h + 1)
                if h < GH - 1:
                    dve.wait_ge(g_done, 2 * h + 3)
                inverse(B[3][:, :], gt[:, :], DV, oinv_done)
                dve.wait_ge(orstd_done, h + 1)
                for v in range(2):
                    link(dve.scalar_tensor_tensor(out=o_acc[:, v, :], in0=o_acc[:, v, :],
                                                  scalar=par[:, G_GN + v:G_GN + v + 1], in1=gt[:, :],
                                                  op0=ALU.mult, op1=ALU.mult))
                    ins = dve.tensor_tensor(go[:, 2 * h + v, :], go[:, 2 * h + v, :], o_acc[:, v, :], ALU.mult)
                ins.then_inc(go_done, 1)

            def scores(h):
                if h == 0:
                    dve.wait_ge(offs_in, 16)
                for i, t in enumerate(SCORE_ORDER):
                    dve.wait_ge(score_done, 4 * h + i + 1)
                    x0 = S - P - t * P
                    ins = dve.tensor_tensor_reduce(out=prob[:, t, :], in0=B[t][:, :], in1=offs[:, x0:x0 + S],
                                                   scale=ASCALE, scalar=-3e38, op0=ALU.add, op1=ALU.max,
                                                   accum_out=stat[:, MX + t:MX + t + 1])
                link(ins)
                dve.tensor_scalar(stat[:, NMX:NMX + ST], stat[:, MX:MX + ST], -1.0, None, ALU.mult)\
                    .then_inc(max_done, 1)

            def pnorm(h):
                dve.wait_ge(p_exp, h + 1)
                link(dve.reciprocal(stat[:, RDEN:RDEN + ST], stat[:, DEN:DEN + ST]))
                for t in range(ST):
                    ins = dve.tensor_scalar(prob[:, t, :], prob[:, t, :], stat[:, RDEN + t:RDEN + t + 1], None, ALU.mult)
                ins.then_inc(p_done, 1)

            def ptrans(h):
                for j in (1, 3):
                    dve.wait_ge(p_turned, 4 * h + j + 1)
                    dve.tensor_copy(probT[:, j, :], B[j][:, :]).then_inc(pt_dve, 1)

            def gla_cat(i):
                for c in (2 * i, 2 * i + 1):
                    dve.wait_ge(xhi_done, KT + c + 1)
                    dve.tensor_tensor(xT_lo[:, c, :], go[:, c, :], xT_hi[:, c, :].bitcast(F32), ALU.subtract)\
                        .then_inc(x_ready, 1)

            def pv(h):
                if h >= 4:
                    dve.wait_ge(xhi_done, KT + AH + h + 1)
                    dve.wait_ge(sq_done, h + 1)
                    dve.scalar_tensor_tensor(out=xT_lo[:, AH + h, :], in0=B[0][:, :],
                                             scalar=par[:, G_AN + h:G_AN + h + 1],
                                             in1=xT_hi[:, AH + h, :].bitcast(F32), op0=ALU.mult, op1=ALU.subtract)\
                        .then_inc(x_ready, 1)

            def attn_cat(i):
                for h in (2 * i, 2 * i + 1):
                    dve.wait_ge(xhi_done, KT + AH + h + 1)
                    dve.scalar_tensor_tensor(out=xT_lo[:, AH + h, :], in0=qT[0][:, h, :],
                                             scalar=par[:, G_AN + h:G_AN + h + 1],
                                             in1=xT_hi[:, AH + h, :].bitcast(F32), op0=ALU.mult, op1=ALU.subtract)\
                        .then_inc(x_ready, 1)

            def attn_sum(_):
                dve.wait_ge(asum_done, 1)
                inverse(B[1][:, 0:ST], stat[:, ARSTD:ARSTD + ST], AW, ainv_done)

            pieces = {"gate": gate, "decay": decay, "keys": keys, "gla_out": gla_out, "gla_norm": gla_norm,
                      "states_a": lambda hd: states(hd, 0), "states_b": lambda hd: states(hd, 1),
                      "scores": scores, "pnorm": pnorm, "ptrans": ptrans, "pv": pv, "gla_cat": gla_cat,
                      "attn_cat": attn_cat, "attn_sum": attn_sum, "rotate": rotate}
            for n in range(FF0):
                if n:
                    split(n + 2, n + 2)
                for piece, arg in SIDE.get(n, ()):
                    if piece in pieces:
                        pieces[piece](arg)
                b, i = divmod(n - WG0, HALF)
                if n >= WG0 and i == HALF - 1:
                    j = b % 4
                    if b < 4:
                        dve.wait_ge(hid_in[j], 16)
                    for s in range(ST):
                        if s == 3:
                            dve.wait_ge(slab_done, n + 1)
                        else:
                            dve.wait_ge(bank_done, 3 * (len(IN_BLOCKS) + b) + s + 1)
                        h = hid[j][:, s, :]
                        if b < 4:
                            dve.tensor_tensor(h, h, A[s][:, :], ALU.add).then_inc(hid_added, 1)
                        else:
                            dve.wait_ge(arstd_done, 1)
                            dve.wait_ge(hid_added, 4 * (b - 4) + s + 1)
                            dve.scalar_tensor_tensor(out=h, in0=A[s][:, :], scalar=stat[:, ARSTD + s:ARSTD + s + 1],
                                                     in1=h, op0=ALU.mult, op1=ALU.add).then_inc(hid_added, 1)

            def row_norm(count, waited):
                dve.wait_ge(waited, count)
                ss = stat[:, SS2:SS2 + 16].rearrange("p (s j) -> p s j", j=4)
                link(dve.tensor_reduce(stat[:, RSTD:RSTD + ST], ss, AX_X, ALU.add))
                inverse(stat[:, RSTD:RSTD + ST], stat[:, RSTD:RSTD + ST], D, inv_done)

            row_norm(ST + 16, ssq_done)
            dve.wait_ge(rstd_done, 2)

            def scale_tile(k):
                if k >= 4:
                    dve.wait_ge(turned, KT + k - 3)
                j, c = divmod(k, 4)
                for s in range(ST):
                    ins = dve.tensor_scalar(hn[k % 4][:, s, :], hid[j][:, s, c * P:(c + 1) * P],
                                            stat[:, RSTD + s:RSTD + s + 1], None, ALU.mult)
                ins.then_inc(hn_done, 1)

            def turned_lo(k):
                dve.wait_ge(xhi_done, 2 * KT + k + 1)
                dve.scalar_tensor_tensor(out=xT_lo[:, k, :], in0=B[k % 4][:, :],
                                         scalar=par[:, G_N2 + k:G_N2 + k + 1],
                                         in1=xT_hi[:, k, :].bitcast(F32), op0=ALU.mult, op1=ALU.subtract)\
                    .then_inc(x_ready, 1)
                if k + 4 < KT:
                    scale_tile(k + 4)

            for k in range(4):
                scale_tile(k)
            for k in range(4):
                turned_lo(k)

            def ffn(order, n0, g, step):
                for i, (what, k) in enumerate(order):
                    n = n0 + i + step * g
                    if what == "gate" and k == 0:
                        src = par[:, NROWS:].rearrange("p (q f) -> p q f", f=FT)[:, :, bass.ds(g * G, G)]
                        if step:
                            dve.wait_ge(conv2, G * g)
                        dve.tensor_copy(gpar[:, :, :], src).then_inc(gpar_done, 1)
                    if not (n0 + i >= LAST0 + len(LAST) - 2 and not step):
                        split(n0 + i + 2, n + 2)
                    if order is FIRST and what == "gate":
                        for t in range(4 + KS * k, min(4 + KS * (k + 1), KT)):
                            turned_lo(t)
                    if what == "gate" and k == NSL - 1:
                        dve.wait_ge(gpar_done, g + 1)
                        for m in range(4):
                            dve.wait_ge(conv1, G * g + m + 1)
                            dve.scalar_tensor_tensor(out=cv[:, m, 1:S], in0=A[m][:, 0:S - 1],
                                                     scalar=gpar[:, 0, m:m + 1], in1=cv[:, m, 1:S],
                                                     op0=ALU.mult, op1=ALU.add).then_inc(conv_first, 1)
                            dve.wait_ge(conv_first, G * g + m + 1)
                            dve.scalar_tensor_tensor(out=cv[:, m, 0:S - 1], in0=A[m][:, 1:S],
                                                     scalar=gpar[:, 2, m:m + 1], in1=cv[:, m, 0:S - 1],
                                                     op0=ALU.mult, op1=ALU.add).then_inc(conv2, 1)
                    if what == "up" and k == NSL - 1:
                        for m in range(4):
                            dve.wait_ge(silu_done, G * g + m + 1)
                            if m == 3:
                                dve.wait_ge(slab_done, n + 1)
                            else:
                                dve.wait_ge(bank_done, bank_base(what, 0, g, step) + m + 1)
                            dve.tensor_tensor(cv[:, m, :], cv[:, m, :], B[m][:, :], ALU.mult).then_inc(act_done, 1)
                        for m in range(4):
                            dve.wait_ge(ahi_done, G * g + m + 1)
                            dve.tensor_tensor(act_lo[:, m, :], cv[:, m, :], act_hi[:, m, :].bitcast(F32), ALU.subtract)\
                                .then_inc(alo_done, 1)
                    if what == "down" and k % 2:
                        j = k // 2
                        banks = B if j % 2 == 0 else A
                        for s in range(ST):
                            if s == 3:
                                dve.wait_ge(slab_done, n + 1)
                            elif step:
                                dve.wait_ge(bank_done, bank_base(what, j, g, step) + s + 1)
                            else:
                                dve.wait_ge(bank_done, bank_base("gate", 0, NG, 1) + 3 * j + s + 1)
                            h = hid[j][:, s, :]
                            dve.tensor_tensor(h, h, banks[s][:, :], ALU.add).then_inc(hid_added, 1)

            ffn(FIRST, FF0, 0, 0)
            with dve.Fori(1, NG) as g:
                ffn(ORDER, LOOP0 - GROUP, g, GROUP)
            ffn(LAST, LAST0, 0, 0)
            row_norm(16, fsq_done)
            dve.wait_ge(rstd_done, 3)
            for s in range(ST):
                dve.wait_ge(gf_done, 8 + s + 1)
                dve.tensor_scalar(hid[2][:, s, :], hid[2][:, s, :], stat[:, RSTD + s:RSTD + s + 1], None, ALU.mult)\
                    .then_inc(fin_done, 1)
            dve.wait_ge(offs_in, 32)
            for s in range(ST):
                h = hid[3][:, s, :]
                dve.scalar_tensor_tensor(out=h, in0=h, scalar=stat[:, RSTD + s:RSTD + s + 1],
                                         in1=gfin[:, 3 * BLK:4 * BLK], op0=ALU.mult, op1=ALU.mult)\
                    .then_inc(fin_done, 1)


_NAMES = ["x", "norm1_g", "w_in", "gf_up", "gf_b", "gb_up", "gb_b", "gla_norm_g", "attn_norm_g", "w_out",
          "norm2_g", "w_gate", "w_up", "conv_w", "conv_b", "w_down", "final_norm_g"]


def kernel(**inputs):
    import concourse.bacc as bacc
    from concourse.bass_utils import run_bass_kernel_spmd

    nc = bacc.Bacc("TRN2", target_bir_lowering=False, num_devices=1)
    arrays = {f"in_{k}": np.ascontiguousarray(inputs[k]) for k in _NAMES}
    arrays.update({f"in_{k}": np.ascontiguousarray(v) for k, v in
                   zip(("tables", "toep", "rope", "masks"), constant_tables())})
    aps = [nc.dram_tensor(k, a.shape, mybir.dt.from_np(a.dtype), kind="ExternalInput").ap() for k, a in arrays.items()]
    out = nc.dram_tensor("out", inputs["x"].shape, F32, kind="ExternalOutput").ap()
    encoder_block(nc, *aps, out)
    r = run_bass_kernel_spmd(nc, [arrays], core_ids=[0])
    return r.results[0]["out"]
```

```python
from contextlib import ExitStack

import concourse.bass as bass
import numpy as np
from concourse import mybir

F32 = mybir.dt.float32
F32R = mybir.dt.float32r
I32 = mybir.dt.int32
ALU = mybir.AluOpType
ACT = mybir.ActivationFunctionType
AX_X = mybir.AxisListType.X

P = 128
S = 512
D = 2048
ST = S // P
KT = D // P
EPS = 1e-6

AW = 1024
AH = 8
HD = AW // AH
ROPE = HD // 4
PATTERNS = ((128, 1), (512, 4), (2048, 16))
THETA = 500000.0
ASCALE = float(HD) ** -0.5

GH = 4
GK = 512
GV = 1024
DK = GK // GH
DV = GV // GH
RANK = 16
CH = 64
NC = S // CH
GSCALE = float(DK) ** -0.5

F = 5632
FT = F // P
G = 4
NG = FT // G

OFF_AQ, OFF_AK, OFF_AV = 0, AW, 2 * AW
OFF_GQ = 3 * AW
OFF_GK, OFF_GV = OFF_GQ + GK, OFF_GQ + 2 * GK
OFF_GR = OFF_GV + GV
OFF_Z = OFF_GR + GV
IN_W = OFF_Z + 2 * RANK

BLK = 512
KS = 2
SLAB = KS * BLK
NSL = KT // KS

IN_BLOCKS = [("gq", OFF_GQ, "f"), ("gk", OFF_GK, "f"), ("gv0", OFF_GV, "t"), ("gr0", OFF_GR, "f"),
             ("gr1", OFF_GR + BLK, "f"), ("gv1", OFF_GV + BLK, "t"),
             ("aq0", OFF_AQ, "f"), ("ak0", OFF_AK, "f"), ("av0", OFF_AV, "t"),
             ("aq1", OFF_AQ + BLK, "f"), ("ak1", OFF_AK + BLK, "f"), ("av1", OFF_AV + BLK, "t")]
Z_SLABS = 2
Z_COL = IN_W - P
Z_KS = KT // Z_SLABS
IN0 = Z_SLABS
WG0 = IN0 + NSL * len(IN_BLOCKS)
HALF = NSL // 2
WA0 = WG0 + HALF * (D // BLK)
FF0 = WA0 + HALF * (D // BLK)
GROUP = 2 * NSL + 2 * (D // BLK)
RING = 3

START = {name: IN0 + NSL * b for b, (name, _, _) in enumerate(IN_BLOCKS)}
BANKS = {name: 1 + 4 * b for b, (name, _, _) in enumerate(IN_BLOCKS)}


def side_pieces():
    side = {}

    def put(n, piece, arg):
        side.setdefault(n, []).append((piece, arg))

    first = START["gv1"] - 11
    for hd in range(2 * GH):
        n = first + 4 * hd
        for k, piece in enumerate(("gate", "decay", "keys", "states_a", "states_b", "gla_out")):
            put(n + k, piece, hd)
        put(n, "gate_log", hd)
        if hd % 2:
            put(n + 6, "gla_norm", hd // 2)
            put(n + 7, "gla_scale", hd // 2)
    for b in range(2):
        for i, name in enumerate((f"aq{b}", f"ak{b}")):
            for m in range(4):
                put(START[name] + NSL + m, "rotate", (b, i, m))
    for h in range(AH):
        n = START["aq1"] - 3 + 6 * h if h < 4 else WG0 - 3 + 4 * (h - 4)
        for k, piece in enumerate(("scores", "pnorm", "ptrans", "pv")):
            put(n + k, piece, h)
    for i in range(HALF):
        put(START["av1"] + i + 1, "gla_cat", i)
    for i in range(2):
        put(WG0, "attn_cat", i)
    put(WA0 - 2, "attn_sum", 0)
    rank = {p: r for r, p in enumerate(("gla_scale", "gla_norm", "attn_cat", "gla_out", "gate", "states_a", "states_b", "gate_log",
                                         "keys", "decay", "pv"))}
    return {n: sorted(v, key=lambda x: rank.get(x[0], 99)) for n, v in side.items()}


SIDE = side_pieces()
NROWS = 2 * KT + AH + 2
G_N1, G_N2, G_AN, G_GN = 0, KT, 2 * KT, 2 * KT + AH
PCOLS = NROWS + 4 * FT
TAP = [NROWS + k * FT for k in range(3)]
CBIAS = NROWS + 3 * FT
TOEP = 2 * S - P
SCORE_ORDER = (1, 2, 3, 0)


def constant_tables():
    t = np.arange(P)
    same = (t[:, None] // CH) == (t[None, :] // CH)
    sums, masks = [], []
    for back in (False, True):
        seen = same & ((t[:, None] >= t[None, :]) if back else (t[:, None] <= t[None, :]))
        b = seen.astype(np.float64) / 16.0
        start = t // CH * CH
        ref = start + (CH // 2 if back else CH // 2 - 1)
        last = start + (0 if back else CH - 1)
        sums += [b - b[:, ref], b, b[:, last] - b]
        masks.append(seen.astype(np.int32))
    x = np.arange(TOEP)[None, :] - (S - P) - t[:, None]
    count = np.zeros(x.shape)
    for window, d in PATTERNS:
        count += (x % d == 0) & (np.abs(x) <= window // 2)
    toep = np.where(count > 0, np.log(np.maximum(count, 1)) / ASCALE, -1e30)
    floats = np.concatenate([np.eye(P)] + sums, axis=1).astype(np.float32)
    half = ROPE // 2
    ang = (np.float32(THETA) ** (-np.arange(0, ROPE, 2, dtype=np.float32) / np.float32(ROPE)))[:, None] \
        * np.arange(S, dtype=np.float32)[None, :]
    ang = ang.astype(np.float32).astype(np.float64)
    cos, sin = np.cos(ang), np.sin(ang)
    rope = np.concatenate([np.concatenate([cos, cos], 0), np.concatenate([-sin, sin], 0)], axis=1)
    assert rope.shape == (2 * half, 2 * S)
    return floats, toep.astype(np.float32), rope.astype(np.float32), np.concatenate(masks, axis=1)


def encoder_block(nc, x, norm1_g, w_in, gf_up, gf_b, gb_up, gb_b, gla_norm_g, attn_norm_g, w_out,
                  norm2_g, w_gate, w_up, conv_w, conv_b, w_down, final_norm_g, tables, toep, rope, masks, out):
    ctx = ExitStack()
    cursor = [(nc.sbuf_base + 31) // 32 * 32]

    def at(name, offset, shape, dt):
        return nc.alloc_sbuf_tensor_at(name, shape, dt, offset=offset)

    def sb(name, shape, dt=F32):
        size = int(np.prod(shape[1:])) * 4
        offset = cursor[0]
        cursor[0] += (size + 31) // 32 * 32
        return at(name, offset, shape, dt)

    with ctx:
        def sem(name):
            return ctx.enter_context(nc.semaphore(name))

        xT_hi = sb("xT_hi", [P, KT, S], F32R)
        xT_lo = sb("xT_lo", [P, KT, S], F32R)
        raw = [sb(f"raw{i}", [P, SLAB]) for i in range(RING)]
        w_hi = [sb(f"w_hi{i}", [P, SLAB], F32R) for i in range(RING)]
        w_lo = [sb(f"w_lo{i}", [P, SLAB], F32R) for i in range(RING)]
        ident_t = sb("ident", [P, P])
        ident = ident_t[:, :]
        sums_t = sb("sums", [P, 6 * P], F32R)
        sums = [sums_t[:, 3 * P * i:3 * P * (i + 1)] for i in range(2)]
        seen = sb("seen", [P, 2 * P], I32)
        ones = sb("ones", [P, P])
        small = sb("small", [P, 2 * S])
        zrope = sb("zrope", [P, S])
        par = sb("par", [P, PCOLS])
        stat = sb("stat", [P, 64])
        gpar = sb("gpar", [P, 4, G])
        KB = 1024
        arena = cursor[0]
        assert arena + 94 * KB <= nc.sbuf_top, (arena, nc.sbuf_top)

        def ar(name, kb, shape, dt=F32):
            return at(name, arena + int(kb * KB), shape, dt)

        xin = [ar(f"xin{s}", 8 * s, [P, D]) for s in range(ST)]
        junk = ar("junk", 64, [P, D])
        prow = ar("prow", 32, [P, 5, P])
        tab = ar("tab", 36, [P, 6 * P])
        gq = ar("gq", 0, [P, GH, S])
        gk = ar("gk", 8, [P, GH, S])
        gv = ar("gv", 16, [P, ST, GV])
        go = ar("go", 32, [P, 2 * GH, S])
        qT = [ar("qT0", 48, [P, 4, S]), ar("qT1", 8, [P, 4, S])]
        kT = [ar("kT0", 56, [P, 4, S]), ar("kT1", 16, [P, 4, S])]
        vv = [ar("vv0", 0, [P, ST, BLK]), ar("vv1", 24, [P, ST, BLK])]
        e = [ar(f"e{i}", 64 + 2 * i, [P, S]) for i in range(4)]
        state = ar("state", 72, [P, NC, DV])
        osq = ar("osq", 72, [P, 2, S])
        kst = ar("kst", 80, [P, ST, P])
        at_m = [ar(f"at_m{i}", 82 + 2 * i, [P, ST, P]) for i in range(2)]
        g_hi = ar("g_hi", 86, [P, S], F32R)
        g_lo = ar("g_lo", 70, [P, S], F32R)
        gt = ar("gt", 88, [P, S])
        o_acc = ar("o_acc", 90, [P, 2, S])
        prob = ar("prob", 64, [P, ST, S])
        probT = ar("probT", 72, [P, ST, S])
        offs = ar("offs", 80, [P, TOEP])
        sq = [ar(f"sq{i}", 84 + 4 * i, [P, S]) for i in range(2)]
        sqsum = ar("sqsum", 86, [P, S])
        hid = [ar("hid0", 56, [P, ST, BLK]), ar("hid1", 0, [P, ST, BLK]),
               ar("hid2", 32, [P, ST, BLK]), ar("hid3", 40, [P, ST, BLK])]
        act_hi = ar("act_hi", 16, [P, G, S], F32R)
        act_lo = ar("act_lo", 24, [P, G, S], F32R)
        cv = ar("cv", 64, [P, G, S])
        hn = [ar(f"hn{i}", at_kb, [P, ST, P]) for i, at_kb in enumerate((72, 74, 86, 88))]
        sqj = ar("sqj", 76, [P, BLK])
        gfin = ar("gfin", 78, [P, D])

        psum = [ctx.enter_context(nc.psum_tensor(name, [P, 4 * BLK], F32)) for name in ("dense", "side")]
        acc = [t[:, b * BLK:(b + 1) * BLK] for t in psum for b in range(4)]
        A, B = acc[:4], acc[4:]
        decays = psum[1][:, :].rearrange("p (t k c) -> p k t c", t=ST, k=4)

        SSQ, RSTD, SS2, MX, NMX, DEN, RDEN, DEC, ARSTD, ORSTD = 0, 4, 8, 24, 28, 32, 36, 40, 48, 52

        tab_in = sem("tab_in")
        offs_in = sem("offs_in")
        x_in = [sem(f"x_in{s}") for s in range(ST)]
        w_in_sem = [sem(f"w_landed{i}") for i in range(RING)]
        hi_done = sem("hi_done")
        lo_done = sem("lo_done")
        slab_done = sem("slab_done")
        bank_done = sem("bank_done")
        down_done = sem("down_done")
        hid_added = sem("hid_added")
        act_chain = sem("act_chain")
        dve_chain = sem("dve_chain")
        pool_init = sem("pool_init")
        pool_chain = sem("pool_chain")
        par_t = sem("par_t")
        par_done = sem("par_done")
        ssq_done = sem("ssq_done")
        inv_done = sem("inv_done")
        rstd_done = sem("rstd_done")
        xn_done = sem("xn_done")
        turned = sem("turned")
        xhi_done = sem("xhi_done")
        x_ready = sem("x_ready")
        gate_pre = sem("gate_pre")
        l_done = sem("l_done")
        g_full = sem("g_full")
        ghi_done = sem("ghi_done")
        g_done = sem("g_done")
        sums_done = sem("sums_done")
        decay_done = sem("decay_done")
        exp_done = sem("exp_done")
        keys_done = sem("keys_done")
        kst_t = sem("kst_t")
        kst_done = sem("kst_done")
        at_done = sem("at_done")
        at_masked = sem("at_masked")
        kv_done = sem("kv_done")
        kv_used = sem("kv_used")
        o_done = sem("o_done")
        o_saved = sem("o_saved")
        osq_done = sem("osq_done")
        osum_done = sem("osum_done")
        oinv_done = sem("oinv_done")
        orstd_done = sem("orstd_done")
        diag_done = sem("diag_done")
        obc_done = sem("obc_done")
        go_done = sem("go_done")
        in_act = sem("in_act")
        rope_done = sem("rope_done")
        score_done = sem("score_done")
        max_done = sem("max_done")
        p_exp = sem("p_exp")
        p_done = sem("p_done")
        p_turned = sem("p_turned")
        pt_act = sem("pt_act")
        pt_dve = sem("pt_dve")
        pv_done = sem("pv_done")
        sq_done = sem("sq_done")
        asum_done = sem("asum_done")
        ainv_done = sem("ainv_done")
        arstd_done = sem("arstd_done")
        gain_in = sem("gain_in")
        gf_done = sem("gf_done")
        fin_act = sem("fin_act")
        sqsum_done = sem("sqsum_done")
        hid_in = [sem(f"hid_in{j}") for j in range(4)]
        hn_done = sem("hn_done")
        conv1 = sem("conv1")
        conv2 = sem("conv2")
        silu_done = sem("silu_done")
        act_done = sem("act_done")
        ahi_done = sem("ahi_done")
        alo_done = sem("alo_done")
        fsq_done = sem("fsq_done")
        fin_done = sem("fin_done")
        stored = sem("stored")
        gpar_done = sem("gpar_done")
        conv_first = sem("conv_first")

        w_in_t = w_in.rearrange("l (t p) n -> p (l t) n", p=P)
        w_out_t = w_out.rearrange("l (t p) n -> p (l t) n", p=P)
        w_gate_t = w_gate.rearrange("l (t p) n -> p (l t) n", p=P)
        w_up_t = w_up.rearrange("l (t p) n -> p (l t) n", p=P)
        w_down_t = w_down.rearrange("l (t p) n -> p (l t) n", p=P)
        x_t = x.rearrange("b (s p) n -> p (b s) n", p=P)
        out_t = out.rearrange("b (s p) n -> p (b s) n", p=P)

        def mixer_slab(n):
            if n < IN0:
                return w_in_t[:, Z_KS * n:Z_KS * (n + 1), Z_COL:Z_COL + P]
            if n < WG0:
                b, i = divmod(n - IN0, NSL)
                c = IN_BLOCKS[b][1]
                return w_in_t[:, KS * i:KS * (i + 1), c:c + BLK]
            b, i = divmod(n - WG0, HALF)
            t = KS * i + (KT // 2 if n < WA0 else 0)
            j = b % (D // BLK)
            return w_out_t[:, t:t + KS, j * BLK:(j + 1) * BLK]

        ORDER = [("gate", i) for i in range(NSL)] + [("down", i) for i in range(2 * (D // BLK))] \
            + [("up", i) for i in range(NSL)]
        FIRST = [w for w in ORDER if w[0] != "down"]
        LAST = [("down", k) for k in (0, 2, 1, 3, 4, 5, 6, 7)]
        PASSES = 2
        PT = ST // PASSES
        LOOP0 = FF0 + len(FIRST)
        LAST0 = LOOP0 + (NG - 1) * GROUP
        assert GROUP % RING == 0

        def ffn_slab(what, i, g):
            if what == "down":
                j, half = divmod(i, 2)
                src = w_down_t[:, bass.ds((g - 1) * G + half * KS, KS), j * BLK:(j + 1) * BLK]
                return src
            src = w_gate_t if what == "gate" else w_up_t
            return src[:, KS * i:KS * (i + 1), bass.ds(g * BLK, BLK)]

        def ksplit(t, n):
            return t.rearrange("p (k c) -> p k c", c=n)

        def last_weights(i):
            if i < 2:
                slot = (LAST0 + i) % RING
                return ksplit(w_hi[slot][:, :], BLK), ksplit(w_lo[slot][:, :], BLK)
            return xT_hi[:, KS * i:KS * (i + 1), :], xT_lo[:, KS * i:KS * (i + 1), :]

        def bank_base(what, j, g, step):
            mixer = 3 * (len(IN_BLOCKS) + 2 * (D // BLK))
            per = 3 * (2 + D // BLK)
            if not step:
                return mixer + (0 if what == "gate" else 3)
            start = mixer + 6 + (g - 1) * per
            if what == "gate":
                return start
            if what == "down":
                return start + 3 + 3 * j
            return start + 3 + 3 * (D // BLK)

        block = ctx.enter_context(nc.Block())

        @block.sync
        def _(sp):
            def load(n0, src, g=0, step=0):
                slot = n0 % RING
                c = src.shape[2]
                if n0 >= RING or step:
                    sp.wait_ge(lo_done, n0 - RING + 1 + step * g)
                sp.dma_start(ksplit(raw[slot][:, :], c), src).then_inc(w_in_sem[slot], 16)

            sp.dma_start(ident, tables[:, 0:P]).then_inc(gain_in, 16)
            for src, r in ((norm1_g, G_N1), (norm2_g, G_N2), (attn_norm_g, G_AN), (gla_norm_g, G_GN)):
                k = src.shape[1] // P
                sp.dma_start(prow[r:r + k, 0, :], src.rearrange("l (r c) -> (l r) c", c=P)).then_inc(gain_in, 16)
            for s in range(ST):
                sp.dma_start(xin[s][:, :], x_t[:, s, :]).then_inc(x_in[s], 16)
            for n in range(FF0):
                load(n, mixer_slab(n))
            for i, (what, k) in enumerate(FIRST):
                load(FF0 + i, ffn_slab(what, k, 0))
            with sp.Fori(1, NG) as g:
                for i, (what, k) in enumerate(ORDER):
                    load(LOOP0 - GROUP + i, ffn_slab(what, k, g), g, GROUP)
            for i, (what, k) in enumerate(LAST):
                load(LAST0 + i, ffn_slab(what, k, NG))
            for p in range(PASSES):
                t = slice(PT * p, PT * (p + 1))
                for q in range(2):
                    for done, j in ((fin_act, q), (fin_done, 2 + q)):
                        sp.wait_ge(done, 2 * PT * p + PT * (q + 1))
                        sp.dma_start(out_t[:, t, j * BLK:(j + 1) * BLK], hid[j][:, t, :]).then_inc(stored, 16)
            sp.wait_ge(stored, 16 * 8)

        @block.gpsimd
        def _(pool):
            for n, (view, value) in enumerate(((ones[:, :], 1.0), (small[64:96, :], 0.0), (zrope[64:96, :], 0.0),
                                               (zrope[64:65, :], 1.0), (small[96:128, :], 0.0))):
                pool.memset(view, value).then_inc(pool_init, 1)
                pool.wait_ge(pool_init, n + 1)
            pool.dma_start(tab[:, :], tables[:, P:]).then_inc(tab_in, 16)
            pool.dma_start(seen[:, :], masks).then_inc(tab_in, 16)
            pool.dma_start(small[0:ROPE, :], rope).then_inc(tab_in, 16)
            for d, (up, bias) in enumerate(((gf_up, gf_b), (gb_up, gb_b))):
                pool.dma_start(small[64:65, d * GK:(d + 1) * GK], bias).then_inc(tab_in, 16)
                pool.dma_start(small[96 + RANK * d:96 + RANK * (d + 1), d * GK:(d + 1) * GK], up[0])\
                    .then_inc(tab_in, 16)
            for k in range(3):
                pool.dma_start(prow[0:FT, 1 + k, :], conv_w[0, k, :].rearrange("(r c) -> r c", c=P))\
                    .then_inc(tab_in, 16)
            pool.dma_start(prow[0:FT, 4, :], conv_b.rearrange("l (r c) -> (l r) c", c=P)).then_inc(tab_in, 16)

            pool.wait_ge(xn_done, ST)
            for i in range(2):
                pool.memset(at_m[i][:, :, :], 0.0).then_inc(pool_init, 1)
                pool.wait_ge(pool_init, 6 + i)
            pool.wait_ge(go_done, GH)
            pool.dma_start(offs[:, :], toep).then_inc(offs_in, 16)
            for h in range(AH):
                pool.wait_ge(sq_done, h + 1)
                if h == 0:
                    pool.tensor_copy(sqsum[:, :], sq[0][:, :]).then_inc(sqsum_done, 1)
                else:
                    pool.wait_ge(sqsum_done, h)
                    pool.tensor_tensor(sqsum[:, :], sqsum[:, :], sq[h % 2][:, :], ALU.add).then_inc(sqsum_done, 1)
                if h == 3:
                    pool.wait_ge(x_ready, KT + 2 * GH)
                    for j in range(4):
                        pool.dma_start(hid[j][:, :, :], x_t[:, :, j * BLK:(j + 1) * BLK]).then_inc(hid_in[j], 16)
            pool.wait_ge(x_ready, 3 * KT)
            pool.dma_start(gfin[:, :], final_norm_g.partition_broadcast(P)).then_inc(offs_in, 16)
            pool.wait_ge(offs_in, 32)
            for p in range(PASSES):
                for j in range(3):
                    for m in range(PT):
                        pool.wait_ge(fsq_done, PT * (4 * p + j) + m + 1)
                        h = hid[j][:, PT * p + m, :]
                        pool.tensor_tensor(h, h, gfin[:, j * BLK:(j + 1) * BLK], ALU.mult).then_inc(gf_done, 1)
                        pool.wait_ge(gf_done, PT * (3 * p + j) + m + 1)

        n_tab = 16 * (3 + 4 + 4)

        IN_BANKS = 1 + 4 * len(IN_BLOCKS)
        OUT_BANKS = 4 * 2 * (D // BLK)
        DOWN_BANKS = 4 * (D // BLK)
        LAST_ADDED = OUT_BANKS + DOWN_BANKS * (NG - 1)

        @block.tensor
        def _(pe):
            def three(o, wh, wl, ah, al, first, last, weights_first):
                for k, (w, a) in enumerate(((wh, ah), (wh, al), (wl, ah))):
                    lhs, rhs = (w, a) if weights_first else (a, w)
                    mm = pe.matmul(o, lhs, rhs, start=first and k == 0, stop=last and k == 2)
                return mm

            def slab(n0, wait, kind, banks, k0, first, last, free=None, inputs=(xT_hi, xT_lo)):
                slot = n0 % RING
                pe.wait_ge(lo_done, wait + 1)
                hi, lo = ksplit(w_hi[slot][:, :], BLK), ksplit(w_lo[slot][:, :], BLK)
                for m in range(4):
                    if first:
                        free(m)
                    c = slice(m * P, (m + 1) * P)
                    for k in range(KS):
                        a, al = inputs[0][:, k0 + k], inputs[1][:, k0 + k]
                        if kind == "f":
                            wh, wl = hi[:, k, c], lo[:, k, c]
                        else:
                            wh, wl, a, al = hi[:, k, :], lo[:, k, :], a[:, c], al[:, c]
                        mm = three(banks[m][:, :], wh, wl, a, al, first and k == 0, last and k == KS - 1, kind == "f")
                    if m == 3:
                        mm.then_inc(slab_done, 1)
                    elif last:
                        mm.then_inc(bank_done, 1)

            def turn_rows(k):
                r, c = (NROWS, 0) if k == 0 else (FT, NROWS + (k - 1) * FT)
                return pe.transpose(B[0][:, c:c + r], prow[0:r, k, :], ident[0:r, 0:r])

            pe.wait_ge(gain_in, 16 * 5)
            turn_rows(0).then_inc(par_t, 1)

            def turn_tile(k, src, seq):
                if seq >= 4:
                    pe.wait_ge(x_ready, seq - 3)
                for s in range(ST):
                    mm = pe.transpose(B[k % 4][:, s * P:(s + 1) * P], src(s), ident)
                mm.then_inc(turned, 1)

            pe.wait_ge(xn_done, ST)
            pe.wait_ge(par_done, 1)

            def turn_x(k):
                turn_tile(k, lambda s: xin[s][:, k * P:(k + 1) * P], k)

            for k in range(4):
                turn_x(k)

            def gate(hd):
                h, d = divmod(hd, 2)
                if hd == 0:
                    pe.wait_ge(sums_done, 1)
                    pe.wait_ge(in_act, 1)
                    pe.wait_ge(par_done, 2)
                if hd >= 3:
                    pe.wait_ge(go_done, (hd - 1) // 2)
                w = small[64:P, d * GK + h * DK:d * GK + (h + 1) * DK]
                for t in range(ST):
                    mm = pe.matmul(B[0][:, t * P:(t + 1) * P], zrope[64:P, t * P:(t + 1) * P], w, start=True, stop=True)
                mm.then_inc(gate_pre, 1)

            def decay(hd):
                d = hd % 2
                pe.wait_ge(g_done, hd + 1)
                if hd:
                    pe.wait_ge(kv_used, 2 * hd)
                for t in (2, 3, 0, 1):
                    if hd and t < 2:
                        pe.wait_ge(o_saved, 2 * (hd - 1) + t + 1)
                    c = slice(t * P, (t + 1) * P)
                    pe.matmul(B[t][:, 0:3 * P], g_hi[:, c], sums[d], start=True, stop=False)
                    mm = pe.matmul(B[t][:, 0:3 * P], g_lo[:, c], sums[d], start=False, stop=True)
                mm.then_inc(decay_done, 1)

            def keys(hd):
                pe.wait_ge(keys_done, hd + 1)
                for t in range(ST):
                    mm = pe.transpose(B[0][:, t * P:(t + 1) * P], e[3][:, t * P:(t + 1) * P], ident)
                mm.then_inc(kst_t, 1)
                for t in range(ST):
                    c = slice(t * P, (t + 1) * P)
                    mm = pe.matmul(B[1][:, c], e[1][:, c], e[0][:, c], start=True, stop=True)
                mm.then_inc(at_done, 1)

            def states(hd, part):
                h, d = divmod(hd, 2)
                if part == 0:
                    pe.wait_ge(kst_done, hd + 1)
                    pe.wait_ge(in_act, BANKS[f"gv{h // 2}"] + 4)
                    if d == 0 and h:
                        pe.wait_ge(oinv_done, h)
                else:
                    pe.wait_ge(kv_used, 2 * hd + 1)
                for i in range(4 - part):
                    step = 4 * part + i
                    c = NC - 1 - step if d else step
                    r = (c % 2) * CH
                    o = B[2 + c % 2][:, (i // 2) * DV:(i // 2 + 1) * DV]
                    mm = pe.matmul(o, kst[r:r + CH, c // 2, :], gv[r:r + CH, c // 2, h * DV:(h + 1) * DV],
                                   start=True, stop=True)
                mm.then_inc(kv_done, 1)

            def gla_out(hd):
                h, d = divmod(hd, 2)
                pe.wait_ge(at_masked, hd + 1)
                pe.wait_ge(kv_used, 2 * hd + 2)
                if hd + 1 < 2 * GH:
                    pe.wait_ge(g_done, hd + 2)
                for v in range(2):
                    for t in range(ST):
                        c = slice(t * P, (t + 1) * P)
                        pe.matmul(B[v][:, c], gv[:, t, h * DV + v * P:h * DV + (v + 1) * P],
                                  at_m[d][:, t, :], start=(t == 0), stop=False, skip_group_check=True)
                    for c in range(NC - 1):
                        c = c if d else c + 1
                        mm = pe.matmul(B[v][:, c * CH:(c + 1) * CH], state[:, c, v * P:(v + 1) * P],
                                       e[2][:, c * CH:(c + 1) * CH], start=False, stop=True, skip_group_check=True)
                    mm.then_inc(o_done, 1)

            def gla_norm(h):
                pe.wait_ge(osq_done, h + 1)
                nxt = 2 * h + 2
                if nxt < 2 * GH:
                    pe.wait_ge(exp_done, nxt + 1)
                for v in range(2):
                    for t in range(ST):
                        mm = pe.matmul(B[3][:, t:t + 1], osq[:, v, t * P:(t + 1) * P], ones[:, 0:1],
                                       start=(v == 0 and t == 0), stop=(v == 1), skip_group_check=True)
                mm.then_inc(osum_done, 1)

            def gla_scale(h):
                pe.wait_ge(diag_done, h + 1)
                if h + 1 < GH:
                    pe.wait_ge(kst_done, 2 * h + 3)
                pe.matmul(B[0][:, :], ones[:, :], osq[:, 0, :], start=True, stop=True).then_inc(obc_done, 1)

            def scores(h):
                b, hh = divmod(h, 4)
                pe.wait_ge(rope_done, 8 * b + 4 + hh + 1)
                if h == 0:
                    pe.wait_ge(go_done, GH)
                else:
                    pe.wait_ge(pt_act, 2 * h)
                    pe.wait_ge(pt_dve, 2 * h)
                for t in SCORE_ORDER:
                    if h and t == 0:
                        pe.wait_ge(sq_done, h)
                        if h > 4:
                            pe.wait_ge(x_ready, KT + 2 * GH + h)
                    pe.matmul(B[t][:, :], qT[b][:, hh, t * P:(t + 1) * P], kT[b][:, hh, :], start=True, stop=True)\
                        .then_inc(score_done, 1)

            def ptrans(h):
                pe.wait_ge(p_done, h + 1)
                for j in range(ST):
                    for t in range(ST):
                        mm = pe.transpose(B[j][:, t * P:(t + 1) * P], prob[:, t, j * P:(j + 1) * P], ident)
                    mm.then_inc(p_turned, 1)

            def pv(h):
                b, hh = divmod(h, 4)
                pe.wait_ge(pt_act, 2 * h + 2)
                pe.wait_ge(pt_dve, 2 * h + 2)
                if hh == 0:
                    pe.wait_ge(in_act, BANKS[f"av{b}"] + 4)
                for j in range(ST):
                    mm = pe.matmul(B[0][:, :], vv[b][:, j, hh * HD:(hh + 1) * HD], probT[:, j, :],
                                   start=(j == 0), stop=(j == ST - 1))
                mm.then_inc(pv_done, 1)

            def attn_sum(_):
                pe.wait_ge(sqsum_done, AH)
                pe.wait_ge(pt_dve, 2 * AH)
                for t in range(ST):
                    mm = pe.matmul(B[1][:, t:t + 1], sqsum[:, t * P:(t + 1) * P], ones[:, 0:1], start=True, stop=True)
                mm.then_inc(asum_done, 1)

            pieces = {"gate": gate, "decay": decay, "keys": keys, "gla_out": gla_out, "gla_norm": gla_norm,
                      "gla_scale": gla_scale,
                      "states_a": lambda hd: states(hd, 0), "states_b": lambda hd: states(hd, 1),
                      "scores": scores, "ptrans": ptrans, "pv": pv, "attn_sum": attn_sum}

            for n in range(FF0):
                if n < IN0:
                    pe.wait_ge(lo_done, n + 1)
                    hi, lo = ksplit(w_hi[n][:, :], P), ksplit(w_lo[n][:, :], P)
                    for k in range(Z_KS):
                        kk = Z_KS * n + k
                        pe.wait_ge(x_ready, kk + 1)
                        if kk + 4 < KT:
                            turn_x(kk + 4)
                        mm = three(A[3][:, :], hi[:, k, :], lo[:, k, :], xT_hi[:, kk, :], xT_lo[:, kk, :],
                                   kk == 0, kk == KT - 1, True)
                    mm.then_inc(slab_done, 1)
                elif n < WG0:
                    b, i = divmod(n - IN0, NSL)
                    if n == IN0 + 2:
                        pe.wait_ge(tab_in, n_tab)
                        for k in range(1, 5):
                            mm = turn_rows(k)
                        mm.then_inc(par_t, 1)

                    def in_free(m):
                        if b:
                            pe.wait_ge(in_act, 1 + 4 * (b - 1) + m + 1)
                        elif m == 3:
                            pe.wait_ge(in_act, 1)

                    slab(n, n, IN_BLOCKS[b][2], A, KS * i, i == 0, i == NSL - 1, in_free)
                else:
                    b, i = divmod(n - WG0, HALF)
                    k0 = KS * i + (0 if n < WA0 else KT // 2)
                    pe.wait_ge(x_ready, KT + k0 + KS)

                    def out_free(m):
                        if b == 0:
                            pe.wait_ge(in_act, IN_BANKS - 3 + m)
                        else:
                            pe.wait_ge(hid_added, 4 * (b - 1) + m + 1)

                    slab(n, n, "t", A, k0, i == 0, i == HALF - 1, out_free)
                for piece, arg in SIDE.get(n, ()):
                    if piece in pieces:
                        pieces[piece](arg)

            def turn_h(k):
                pe.wait_ge(hn_done, k + 1)
                turn_tile(k, lambda s: hn[k % 4][:, s, :], 2 * KT + k)

            for k in range(4):
                turn_h(k)

            def ffn(order, n0, g, step, opening):
                added = OUT_BANKS + DOWN_BANKS * (g - 1)
                for i, (what, k) in enumerate(order):
                    n = n0 + i + step * g
                    if what == "down":
                        j, half = divmod(k, 2)
                        if k < 2:
                            pe.wait_ge(alo_done, G * g - (0 if k else KS))

                        def free(m):
                            if j == 0:
                                pe.wait_ge(act_done, G * (g - 1) + m + 1)
                            elif j == 1:
                                pe.wait_ge(conv2, G * g + m + 1)
                            else:
                                pe.wait_ge(hid_added, added + 4 * (j - 2) + m + 1)

                        slab(n0 + i, n, "t", B if j % 2 == 0 else A, half * KS, half == 0, half == 1, free,
                             (act_hi, act_lo))
                    elif what == "gate":
                        if opening == "first":
                            pe.wait_ge(x_ready, 2 * KT + KS * (k + 1))
                            for t in range(4 + KS * k, min(4 + KS * (k + 1), KT)):
                                turn_h(t)

                        def free(m):
                            if opening == "first":
                                pe.wait_ge(hid_added, OUT_BANKS - 4 + m + 1)
                            else:
                                pe.wait_ge(conv2, G * (g - 1) + m + 1)
                                pe.wait_ge(hid_added, added - 4 + m + 1)

                        slab(n0 + i, n, "f", A, KS * k, k == 0, k == NSL - 1, free)
                    else:
                        def free(m):
                            if opening == "first":
                                pe.wait_ge(x_ready, 3 * KT)
                            else:
                                pe.wait_ge(hid_added, added + 8 + m + 1)

                        slab(n0 + i, n, "f", B, KS * k, k == 0, k == NSL - 1, free)

            ffn(FIRST, FF0, 0, 0, "first")
            with pe.Fori(1, NG) as g:
                ffn(ORDER, LOOP0 - GROUP, g, GROUP, "loop")
            for p in range(PASSES):
                for i, (_, k) in enumerate(LAST):
                    j, half = divmod(k, 2)
                    q = 4 * p + j
                    if p == 0:
                        pe.wait_ge(lo_done, LAST0 + i + 1)
                        if i in (0, 2):
                            pe.wait_ge(alo_done, G * NG - (0 if i else KS))
                    hi, lo = last_weights(i)
                    for m in range(PT):
                        if half == 0:
                            if q >= 4:
                                pe.wait_ge(hid_added, LAST_ADDED + PT * (q - 4) + m + 1)
                            elif q >= 2:
                                pe.wait_ge(act_done, G * (NG - 1) + PT * (q - 2) + m + 1)
                            else:
                                pe.wait_ge(hid_added, LAST_ADDED - 4 + PT * q + m + 1)
                        c = slice((PT * p + m) * P, (PT * p + m + 1) * P)
                        for kk in range(KS):
                            t = half * KS + kk
                            mm = three(acc[PT * (q % 4) + m][:, :], hi[:, kk, :], lo[:, kk, :],
                                       act_hi[:, t, c], act_lo[:, t, c],
                                       half == 0 and kk == 0, half == 1 and kk == KS - 1, False)
                        if half == 1:
                            mm.then_inc(down_done, 1)

        @block.scalar
        def _(act):
            chain = [0]

            def link(ins):
                chain[0] += 1
                ins.then_inc(act_chain, 1)
                act.wait_ge(act_chain, chain[0])

            def split(n0, wait, g8):
                slot = n0 % RING
                act.wait_ge(w_in_sem[slot], 16 * (n0 // RING + 1) + 16 * g8)
                if n0 >= RING:
                    act.wait_ge(slab_done, wait - RING + 1)
                act.activation(w_hi[slot][:, :], raw[slot][:, :], ACT.Copy).then_inc(hi_done, 1)

            act.wait_ge(par_t, 1)
            act.activation(par[:, 0:NROWS], B[0][:, 0:NROWS], ACT.Copy).then_inc(par_done, 1)
            for s in range(ST):
                act.wait_ge(x_in[s], 16)
                if s:
                    act.wait_ge(ssq_done, s)
                act.activation(junk[:, :], xin[s][:, :], ACT.Square, accum_out=stat[:, SSQ + s:SSQ + s + 1])\
                    .then_inc(ssq_done, 1)
                act.wait_ge(inv_done, s + 1)
                act.activation(stat[:, RSTD + s:RSTD + s + 1], stat[:, RSTD + s:RSTD + s + 1], ACT.Sqrt)\
                    .then_inc(rstd_done, 1)
            act.wait_ge(par_done, 1)
            split(0, 0, 0)
            split(1, 1, 0)

            def tile_hi(k, g0, seq):
                act.wait_ge(turned, seq + 1)
                act.activation(xT_hi[:, k, :], B[k % 4][:, :], ACT.Copy, scale=par[:, g0 + k:g0 + k + 1])\
                    .then_inc(xhi_done, 1)

            for k in range(KT):
                tile_hi(k, G_N1, k)
                if k == KT // 2:
                    split(2, 2, 0)

            def evac_in(n):
                if n == IN0 - 1:
                    act.wait_ge(slab_done, IN0)
                    act.activation(zrope[96:P, :], A[3][96:P, :], ACT.Copy).then_inc(in_act, 1)
                    return
                b, i = divmod(n - IN0, NSL)
                if n < IN0 or n >= WG0 or i != NSL - 1:
                    return
                name = IN_BLOCKS[b][0]
                if name in ("av0", "aq1", "ak1", "av1"):
                    act.wait_ge(go_done, GH)
                for m in range(4):
                    if m == 3:
                        act.wait_ge(slab_done, n + 1)
                    else:
                        act.wait_ge(bank_done, 3 * b + m + 1)
                    src, fn, scale = A[m][:, :], ACT.Copy, 1.0
                    if name == "gq":
                        dst, scale = gq[:, m, :], GSCALE
                    elif name == "gk":
                        dst = gk[:, m, :]
                    elif name[:2] == "gr":
                        dst, fn = go[:, 4 * int(name[2]) + m, :], ACT.Silu
                    elif name[:2] == "gv":
                        v = int(name[2])
                        dst = gv[:, m, v * BLK:(v + 1) * BLK]
                    elif name[:2] == "aq":
                        dst = qT[int(name[2])][:, m, :]
                    elif name[:2] == "ak":
                        dst = kT[int(name[2])][:, m, :]
                    else:
                        dst = vv[int(name[2])][:, m, :]
                    act.activation(dst, src, fn, scale=scale).then_inc(in_act, 1)

            def gate(hd):
                act.wait_ge(gate_pre, hd + 1)
                if hd:
                    act.wait_ge(g_done, hd)
                link(act.activation(gt[:, :], B[0][:, :], ACT.Abs))
                link(act.activation(gt[:, :], gt[:, :], ACT.Exp, scale=-1.0))
                act.activation(gt[:, :], gt[:, :], ACT.Ln, bias=1.0).then_inc(l_done, 1)
                act.wait_ge(g_full, hd + 1)
                if hd:
                    act.wait_ge(decay_done, hd)
                act.activation(g_hi[:, :], gt[:, :], ACT.Copy).then_inc(ghi_done, 1)

            def decay(hd):
                act.wait_ge(decay_done, hd + 1)
                if hd:
                    act.wait_ge(o_done, 2 * hd)
                d = hd % 2

                def tiles(t):
                    return t[:, :].rearrange("p (t c) -> p t c", c=P)

                act.activation(tiles(e[0]), decays[:, 0], ACT.Exp)
                act.activation(tiles(e[1]), decays[:, 0], ACT.Exp, scale=-1.0)
                act.activation(tiles(e[2]), decays[:, 1], ACT.Exp)
                last = decays[:, 1].rearrange("p t (c x) -> p t c x", x=CH)[:, :, :, 0 if d else CH - 1]
                act.activation(stat[:, DEC:DEC + NC].rearrange("p (t c) -> p t c", t=ST), last, ACT.Exp)
                act.activation(tiles(e[3]), decays[:, 2], ACT.Exp).then_inc(exp_done, 1)

            def keys(hd):
                act.wait_ge(kst_t, hd + 1)
                act.activation(kst[:, :, :], B[0][:, :].rearrange("p (t k) -> p t k", k=P), ACT.Copy)\
                    .then_inc(kst_done, 1)

            def gla_out(hd):
                if hd % 2:
                    h = hd // 2
                    act.wait_ge(o_saved, 2 * (hd + 1))
                    for v in range(2):
                        ins = act.activation(osq[:, v, :], o_acc[:, v, :], ACT.Square)
                    ins.then_inc(osq_done, 1)

            def gla_norm(h):
                act.wait_ge(oinv_done, h + 1)
                act.activation(stat[:, ORSTD:ORSTD + ST], stat[:, ORSTD:ORSTD + ST], ACT.Sqrt).then_inc(orstd_done, 1)

            def scores(h):
                act.wait_ge(max_done, h + 1)
                for t in range(ST):
                    ins = act.activation(prob[:, t, :], prob[:, t, :], ACT.Exp, bias=stat[:, NMX + t:NMX + t + 1],
                                         accum_out=stat[:, DEN + t:DEN + t + 1])
                ins.then_inc(p_exp, 1)

            def ptrans(h):
                for j in (0, 2):
                    act.wait_ge(p_turned, 4 * h + j + 1)
                    act.activation(probT[:, j, :], B[j][:, :], ACT.Copy).then_inc(pt_act, 1)

            def pv(h):
                act.wait_ge(pv_done, h + 1)
                if h < 4:
                    act.activation(qT[0][:, h, :], B[0][:, :], ACT.Copy)
                else:
                    act.activation(xT_hi[:, AH + h, :], B[0][:, :], ACT.Copy, scale=par[:, G_AN + h:G_AN + h + 1])\
                        .then_inc(xhi_done, 1)
                if h >= 2:
                    act.wait_ge(sqsum_done, h - 1)
                act.activation(sq[h % 2][:, :], B[0][:, :], ACT.Square).then_inc(sq_done, 1)

            def gla_cat(i):
                act.wait_ge(slab_done, START["av1"] + i + 1)
                for c in (2 * i, 2 * i + 1):
                    act.activation(xT_hi[:, c, :], go[:, c, :], ACT.Copy).then_inc(xhi_done, 1)

            def attn_cat(i):
                act.wait_ge(slab_done, WG0)
                for h in (2 * i, 2 * i + 1):
                    act.activation(xT_hi[:, AH + h, :], qT[0][:, h, :], ACT.Copy, scale=par[:, G_AN + h:G_AN + h + 1])\
                        .then_inc(xhi_done, 1)

            def attn_sum(_):
                act.wait_ge(ainv_done, 1)
                act.activation(stat[:, ARSTD:ARSTD + ST], stat[:, ARSTD:ARSTD + ST], ACT.Sqrt).then_inc(arstd_done, 1)

            pieces = {"gate": gate, "decay": decay, "keys": keys, "gla_out": gla_out, "gla_norm": gla_norm, 
                      "scores": scores, "ptrans": ptrans, "pv": pv, "gla_cat": gla_cat, "attn_cat": attn_cat,
                      "attn_sum": attn_sum}
            for n in range(FF0):
                if n:
                    split(n + 2, n + 2, 0)
                if n == IN0 + 2:
                    act.wait_ge(par_t, 2)
                    act.activation(par[:, NROWS:], B[0][:, NROWS:PCOLS], ACT.Copy).then_inc(par_done, 1)
                evac_in(n)
                for piece, arg in SIDE.get(n, ()):
                    if piece in pieces:
                        pieces[piece](arg)
                if n >= WA0 and (n - WA0) % HALF == HALF - 1:
                    j = (n - WA0) // HALF
                    for s in range(ST):
                        act.wait_ge(hid_added, OUT_BANKS // 2 + 4 * j + s + 1)
                        act.activation(sqj[:, :], hid[j][:, s, :], ACT.Square,
                                       accum_out=stat[:, SS2 + 4 * s + j:SS2 + 4 * s + j + 1]).then_inc(ssq_done, 1)
                        act.wait_ge(ssq_done, ST + 4 * j + s + 1)
            act.wait_ge(inv_done, ST + 1)
            act.activation(stat[:, RSTD:RSTD + ST], stat[:, RSTD:RSTD + ST], ACT.Sqrt).then_inc(rstd_done, 1)
            for k in range(4):
                tile_hi(k, G_N2, KT + k)

            def ffn(order, n0, g, step):
                for i, (what, k) in enumerate(order):
                    n = n0 + i + step * g
                    split(n0 + i + 2, n + 2, (step // RING) * g)
                    if order is FIRST and what == "gate":
                        for t in range(4 + KS * k, min(4 + KS * (k + 1), KT)):
                            tile_hi(t, G_N2, KT + t)
                    if what == "gate" and k == NSL - 1:
                        for m in range(4):
                            act.wait_ge(gpar_done, g + 1)
                            if m == 3:
                                act.wait_ge(slab_done, n + 1)
                            else:
                                act.wait_ge(bank_done, bank_base(what, 0, g, step) + m + 1)
                            if step:
                                act.wait_ge(alo_done, G * g - G + m + 1)
                            act.activation(cv[:, m, :], A[m][:, :], ACT.Identity, bias=gpar[:, 3, m:m + 1],
                                           scale=gpar[:, 1, m:m + 1]).then_inc(conv1, 1)
                        for m in range(4):
                            act.wait_ge(conv2, G * g + m + 1)
                            act.activation(cv[:, m, :], cv[:, m, :], ACT.Silu).then_inc(silu_done, 1)
                    if what == "up" and k == NSL - 1:
                        for m in range(4):
                            act.wait_ge(act_done, G * g + m + 1)
                            act.activation(act_hi[:, m, :], cv[:, m, :], ACT.Copy).then_inc(ahi_done, 1)

            ffn(FIRST, FF0, 0, 0)
            with act.Fori(1, NG) as g:
                ffn(ORDER, LOOP0 - GROUP, g, GROUP)
            def last_hi(i):
                n = LAST0 + i
                act.wait_ge(w_in_sem[n % RING], 16 * (n // RING + 1))
                if i == 2:
                    act.wait_ge(slab_done, LAST0)
                act.activation(last_weights(i)[0], ksplit(raw[n % RING][:, :], BLK), ACT.Copy).then_inc(hi_done, 1)

            def final_squares(q):
                p, j = divmod(q, 4)
                for m in range(PT):
                    s = PT * p + m
                    act.wait_ge(hid_added, LAST_ADDED + PT * q + m + 1)
                    act.activation(sqj[:, :], hid[j][:, s, :], ACT.Square,
                                   accum_out=stat[:, SS2 + 4 * s + j:SS2 + 4 * s + j + 1]).then_inc(fsq_done, 1)
                    act.wait_ge(fsq_done, PT * q + m + 1)

            def final_scale(p):
                r = stat[:, RSTD + PT * p:RSTD + PT * (p + 1)]
                act.wait_ge(inv_done, ST + 1 + p + 1)
                act.activation(r, r, ACT.Sqrt).then_inc(rstd_done, 1)
                act.wait_ge(rstd_done, ST + 1 + p + 1)
                for j in range(2):
                    for m in range(PT):
                        s = PT * p + m
                        act.wait_ge(gf_done, PT * (3 * p + j) + m + 1)
                        act.activation(hid[j][:, s, :], hid[j][:, s, :], ACT.Copy,
                                       scale=stat[:, RSTD + s:RSTD + s + 1]).then_inc(fin_act, 1)

            for i, (_, k) in enumerate(LAST):
                if i + 2 < len(LAST):
                    last_hi(i + 2)
                if k % 2:
                    final_squares(k // 2)
            for p in range(PASSES):
                if p:
                    for j in range(4):
                        final_squares(4 * p + j)
                final_scale(p)

        @block.vector
        def _(dve):
            chain = [0]

            def link(ins):
                chain[0] += 1
                ins.then_inc(dve_chain, 1)
                dve.wait_ge(dve_chain, chain[0])

            def split(n0, wait):
                slot = n0 % RING
                dve.wait_ge(hi_done, wait + 1)
                dve.tensor_tensor(w_lo[slot][:, :], raw[slot][:, :], w_hi[slot][:, :].bitcast(F32), ALU.subtract)\
                    .then_inc(lo_done, 1)

            def inverse(src, dst, width, waited):
                link(dve.tensor_scalar(dst, src, 1.0 / width, EPS, ALU.mult, ALU.add))
                dve.reciprocal(dst, dst).then_inc(waited, 1)

            for s in range(ST):
                dve.wait_ge(ssq_done, s + 1)
                inverse(stat[:, SSQ + s:SSQ + s + 1], stat[:, RSTD + s:RSTD + s + 1], D, inv_done)
                dve.wait_ge(rstd_done, s + 1)
                dve.tensor_scalar(xin[s][:, :], xin[s][:, :], stat[:, RSTD + s:RSTD + s + 1], None, ALU.mult)\
                    .then_inc(xn_done, 1)

            def tile_lo(k, g0, seq):
                dve.wait_ge(xhi_done, seq + 1)
                dve.scalar_tensor_tensor(out=xT_lo[:, k, :], in0=B[k % 4][:, :], scalar=par[:, g0 + k:g0 + k + 1],
                                         in1=xT_hi[:, k, :].bitcast(F32), op0=ALU.mult, op1=ALU.subtract)\
                    .then_inc(x_ready, 1)

            split(0, 0)
            split(1, 1)
            dve.wait_ge(par_done, 1)
            for k in range(KT):
                tile_lo(k, G_N1, k)
                if k == KT // 2:
                    split(2, 2)
            dve.wait_ge(tab_in, n_tab)
            dve.tensor_copy(sums_t[:, :], tab[:, :]).then_inc(sums_done, 1)

            swap = [(r + ROPE // 2) % ROPE for r in range(ROPE)]

            def rotate(arg):
                b, i, m = arg
                dve.wait_ge(in_act, BANKS[("aq", "ak")[i] + str(b)] + m + 1)
                src = (qT, kT)[i][b][0:ROPE, m, :]
                if rotated:
                    dve.wait_ge(rope_done, len(rotated))
                rotated.append(arg)
                link(dve.stream_shuffle(zrope[0:ROPE, :], src, swap))
                dve.tensor_tensor(zrope[0:ROPE, :], zrope[0:ROPE, :], small[0:ROPE, S:2 * S], ALU.mult)
                link(dve.tensor_tensor(src, src, small[0:ROPE, 0:S], ALU.mult))
                dve.tensor_tensor(src, src, zrope[0:ROPE, :], ALU.add).then_inc(rope_done, 1)

            rotated = []

            def gate_log(hd):
                dve.wait_ge(l_done, hd + 1)
                dve.scalar_tensor_tensor(out=gt[:, :], in0=B[0][:, :], scalar=0.0,
                                         in1=gt[:, :], op0=ALU.min, op1=ALU.subtract).then_inc(g_full, 1)
                dve.wait_ge(ghi_done, hd + 1)
                dve.wait_ge(g_full, hd + 1)
                dve.tensor_tensor(g_lo[:, :], gt[:, :], g_hi[:, :].bitcast(F32), ALU.subtract).then_inc(g_done, 1)

            def decay(hd):
                h = hd // 2
                dve.wait_ge(exp_done, hd + 1)
                dve.wait_ge(in_act, BANKS["gk"] + 4)
                for i, src in enumerate((gq, gk, gq, gk)):
                    ins = dve.tensor_tensor(e[i][:, :], e[i][:, :], src[:, h, :], ALU.mult)
                ins.then_inc(keys_done, 1)

            def keys(hd):
                d = hd % 2
                dve.wait_ge(at_done, hd + 1)
                if hd == 0:
                    dve.wait_ge(pool_init, 7)
                mask = seen[:, d * P:(d + 1) * P]
                for t in range(ST):
                    ins = dve.copy_predicated(at_m[d][:, t, :], mask, B[1][:, t * P:(t + 1) * P])
                ins.then_inc(at_masked, 1)

            def states(hd, part):
                d = hd % 2
                dve.wait_ge(kv_done, 2 * hd + part + 1)
                for i in range(4):
                    step = 4 * part + i
                    c = NC - 1 - step if d else step
                    nxt = c - 1 if d else c + 1
                    kv = B[2 + c % 2][:, (i // 2) * DV:(i // 2 + 1) * DV]
                    if step == 0:
                        link(dve.tensor_copy(state[:, nxt, :], kv))
                    elif step < NC - 1:
                        ins = dve.scalar_tensor_tensor(out=state[:, nxt, :], in0=state[:, c, :],
                                                       scalar=stat[:, DEC + c:DEC + c + 1], in1=kv,
                                                       op0=ALU.mult, op1=ALU.add)
                        if i == 3 or step == NC - 2:
                            ins.then_inc(kv_used, 1)
                            dve.wait_ge(kv_used, 2 * hd + part + 1)
                        else:
                            link(ins)

            def gla_out(hd):
                d = hd % 2
                for v in range(2):
                    dve.wait_ge(o_done, 2 * hd + v + 1)
                    if d == 0:
                        ins = dve.tensor_copy(o_acc[:, v, :], B[v][:, :])
                    else:
                        ins = dve.tensor_tensor(o_acc[:, v, :], o_acc[:, v, :], B[v][:, :], ALU.add)
                    ins.then_inc(o_saved, 1)

            def gla_norm(h):
                dve.wait_ge(osum_done, h + 1)
                inverse(B[3][:, 0:ST], stat[:, ORSTD:ORSTD + ST], DV, oinv_done)
                dve.wait_ge(orstd_done, h + 1)
                for t in range(ST):
                    ins = dve.tensor_scalar(osq[:, 0, t * P:(t + 1) * P], ident, stat[:, ORSTD + t:ORSTD + t + 1], None,
                                            ALU.mult)
                ins.then_inc(diag_done, 1)

            def gla_scale(h):
                dve.wait_ge(obc_done, h + 1)
                for v in range(2):
                    ins = dve.scalar_tensor_tensor(out=o_acc[:, v, :], in0=o_acc[:, v, :],
                                                   scalar=par[:, G_GN + v:G_GN + v + 1], in1=B[0][:, :],
                                                   op0=ALU.mult, op1=ALU.mult)
                link(ins)
                for v in range(2):
                    ins = dve.tensor_tensor(go[:, 2 * h + v, :], go[:, 2 * h + v, :], o_acc[:, v, :], ALU.mult)
                ins.then_inc(go_done, 1)

            def scores(h):
                if h == 0:
                    dve.wait_ge(offs_in, 16)
                for i, t in enumerate(SCORE_ORDER):
                    dve.wait_ge(score_done, 4 * h + i + 1)
                    x0 = S - P - t * P
                    ins = dve.tensor_tensor_reduce(out=prob[:, t, :], in0=B[t][:, :], in1=offs[:, x0:x0 + S],
                                                   scale=ASCALE, scalar=-3e38, op0=ALU.add, op1=ALU.max,
                                                   accum_out=stat[:, MX + t:MX + t + 1])
                link(ins)
                dve.tensor_scalar(stat[:, NMX:NMX + ST], stat[:, MX:MX + ST], -1.0, None, ALU.mult)\
                    .then_inc(max_done, 1)

            def pnorm(h):
                dve.wait_ge(p_exp, h + 1)
                link(dve.reciprocal(stat[:, RDEN:RDEN + ST], stat[:, DEN:DEN + ST]))
                for t in range(ST):
                    ins = dve.tensor_scalar(prob[:, t, :], prob[:, t, :], stat[:, RDEN + t:RDEN + t + 1], None, ALU.mult)
                ins.then_inc(p_done, 1)

            def ptrans(h):
                for j in (1, 3):
                    dve.wait_ge(p_turned, 4 * h + j + 1)
                    dve.tensor_copy(probT[:, j, :], B[j][:, :]).then_inc(pt_dve, 1)

            def gla_cat(i):
                for c in (2 * i, 2 * i + 1):
                    dve.wait_ge(xhi_done, KT + c + 1)
                    dve.tensor_tensor(xT_lo[:, c, :], go[:, c, :], xT_hi[:, c, :].bitcast(F32), ALU.subtract)\
                        .then_inc(x_ready, 1)

            def pv(h):
                if h >= 4:
                    dve.wait_ge(xhi_done, KT + AH + h + 1)
                    dve.wait_ge(sq_done, h + 1)
                    dve.scalar_tensor_tensor(out=xT_lo[:, AH + h, :], in0=B[0][:, :],
                                             scalar=par[:, G_AN + h:G_AN + h + 1],
                                             in1=xT_hi[:, AH + h, :].bitcast(F32), op0=ALU.mult, op1=ALU.subtract)\
                        .then_inc(x_ready, 1)

            def attn_cat(i):
                for h in (2 * i, 2 * i + 1):
                    dve.wait_ge(xhi_done, KT + AH + h + 1)
                    dve.scalar_tensor_tensor(out=xT_lo[:, AH + h, :], in0=qT[0][:, h, :],
                                             scalar=par[:, G_AN + h:G_AN + h + 1],
                                             in1=xT_hi[:, AH + h, :].bitcast(F32), op0=ALU.mult, op1=ALU.subtract)\
                        .then_inc(x_ready, 1)

            def attn_sum(_):
                dve.wait_ge(asum_done, 1)
                inverse(B[1][:, 0:ST], stat[:, ARSTD:ARSTD + ST], AW, ainv_done)

            pieces = {"gate_log": gate_log, "decay": decay, "keys": keys, "gla_out": gla_out, "gla_norm": gla_norm,
                      "gla_scale": gla_scale,
                      "states_a": lambda hd: states(hd, 0), "states_b": lambda hd: states(hd, 1),
                      "scores": scores, "pnorm": pnorm, "ptrans": ptrans, "pv": pv, "gla_cat": gla_cat,
                      "attn_cat": attn_cat, "attn_sum": attn_sum, "rotate": rotate}
            for n in range(FF0):
                if n:
                    split(n + 2, n + 2)
                b, i = divmod(n - WG0, HALF)
                if n >= WG0 and i == HALF - 1:
                    j = b % 4
                    if b < 4:
                        dve.wait_ge(hid_in[j], 16)
                    for s in range(ST):
                        if s == 3:
                            dve.wait_ge(slab_done, n + 1)
                        else:
                            dve.wait_ge(bank_done, 3 * (len(IN_BLOCKS) + b) + s + 1)
                        h = hid[j][:, s, :]
                        if b < 4:
                            dve.tensor_tensor(h, h, A[s][:, :], ALU.add).then_inc(hid_added, 1)
                        else:
                            dve.wait_ge(arstd_done, 1)
                            dve.wait_ge(hid_added, 4 * (b - 4) + s + 1)
                            dve.scalar_tensor_tensor(out=h, in0=A[s][:, :], scalar=stat[:, ARSTD + s:ARSTD + s + 1],
                                                     in1=h, op0=ALU.mult, op1=ALU.add).then_inc(hid_added, 1)
                for piece, arg in SIDE.get(n, ()):
                    if piece in pieces:
                        pieces[piece](arg)

            def row_norm(s0, tiles):
                ss = stat[:, SS2 + 4 * s0:SS2 + 4 * (s0 + tiles)].rearrange("p (s j) -> p s j", j=4)
                r = stat[:, RSTD + s0:RSTD + s0 + tiles]
                link(dve.tensor_reduce(r, ss, AX_X, ALU.add))
                inverse(r, r, D, inv_done)

            dve.wait_ge(ssq_done, ST + 16)
            row_norm(0, ST)
            dve.wait_ge(rstd_done, ST + 1)

            def scale_tile(k):
                if k >= 4:
                    dve.wait_ge(turned, KT + k - 3)
                j, c = divmod(k, 4)
                for s in range(ST):
                    ins = dve.tensor_scalar(hn[k % 4][:, s, :], hid[j][:, s, c * P:(c + 1) * P],
                                            stat[:, RSTD + s:RSTD + s + 1], None, ALU.mult)
                ins.then_inc(hn_done, 1)

            def turned_lo(k):
                dve.wait_ge(xhi_done, 2 * KT + k + 1)
                dve.scalar_tensor_tensor(out=xT_lo[:, k, :], in0=B[k % 4][:, :],
                                         scalar=par[:, G_N2 + k:G_N2 + k + 1],
                                         in1=xT_hi[:, k, :].bitcast(F32), op0=ALU.mult, op1=ALU.subtract)\
                    .then_inc(x_ready, 1)
                if k + 4 < KT:
                    scale_tile(k + 4)

            for k in range(4):
                scale_tile(k)
            for k in range(4):
                turned_lo(k)

            def ffn(order, n0, g, step):
                for i, (what, k) in enumerate(order):
                    n = n0 + i + step * g
                    if what == "gate" and k == 0:
                        src = par[:, NROWS:].rearrange("p (q f) -> p q f", f=FT)[:, :, bass.ds(g * G, G)]
                        if step:
                            dve.wait_ge(conv2, G * g)
                        dve.tensor_copy(gpar[:, :, :], src).then_inc(gpar_done, 1)
                    split(n0 + i + 2, n + 2)
                    if order is FIRST and what == "gate":
                        for t in range(4 + KS * k, min(4 + KS * (k + 1), KT)):
                            turned_lo(t)
                    if what == "gate" and k == NSL - 1:
                        dve.wait_ge(gpar_done, g + 1)
                        for m in range(4):
                            dve.wait_ge(conv1, G * g + m + 1)
                            dve.scalar_tensor_tensor(out=cv[:, m, 1:S], in0=A[m][:, 0:S - 1],
                                                     scalar=gpar[:, 0, m:m + 1], in1=cv[:, m, 1:S],
                                                     op0=ALU.mult, op1=ALU.add).then_inc(conv_first, 1)
                            dve.wait_ge(conv_first, G * g + m + 1)
                            dve.scalar_tensor_tensor(out=cv[:, m, 0:S - 1], in0=A[m][:, 1:S],
                                                     scalar=gpar[:, 2, m:m + 1], in1=cv[:, m, 0:S - 1],
                                                     op0=ALU.mult, op1=ALU.add).then_inc(conv2, 1)
                    if what == "up" and k == NSL - 1:
                        for m in range(5):
                            if m < 4:
                                dve.wait_ge(silu_done, G * g + m + 1)
                                if m == 3:
                                    dve.wait_ge(slab_done, n + 1)
                                else:
                                    dve.wait_ge(bank_done, bank_base(what, 0, g, step) + m + 1)
                                dve.tensor_tensor(cv[:, m, :], cv[:, m, :], B[m][:, :], ALU.mult).then_inc(act_done, 1)
                            if m:
                                dve.wait_ge(ahi_done, G * g + m)
                                dve.tensor_tensor(act_lo[:, m - 1, :], cv[:, m - 1, :],
                                                  act_hi[:, m - 1, :].bitcast(F32), ALU.subtract).then_inc(alo_done, 1)
                    if what == "down" and k % 2:
                        j = k // 2
                        banks = B if j % 2 == 0 else A
                        for s in range(ST):
                            if s == 3:
                                dve.wait_ge(slab_done, n + 1)
                            else:
                                dve.wait_ge(bank_done, bank_base(what, j, g, step) + s + 1)
                            h = hid[j][:, s, :]
                            dve.tensor_tensor(h, h, banks[s][:, :], ALU.add).then_inc(hid_added, 1)

            ffn(FIRST, FF0, 0, 0)
            with dve.Fori(1, NG) as g:
                ffn(ORDER, LOOP0 - GROUP, g, GROUP)
            def last_lo(i):
                hi, lo = last_weights(i)
                dve.wait_ge(hi_done, LAST0 + i + 1)
                dve.tensor_tensor(lo, ksplit(raw[(LAST0 + i) % RING][:, :], BLK), hi.bitcast(F32), ALU.subtract)\
                    .then_inc(lo_done, 1)

            def last_add(q):
                p, j = divmod(q, 4)
                for m in range(PT):
                    dve.wait_ge(down_done, PT * q + m + 1)
                    h = hid[j][:, PT * p + m, :]
                    dve.tensor_tensor(h, h, acc[PT * j + m][:, :], ALU.add).then_inc(hid_added, 1)

            def final_scale(p):
                dve.wait_ge(fsq_done, 4 * PT * (p + 1))
                row_norm(PT * p, PT)
                dve.wait_ge(rstd_done, ST + 1 + p + 1)
                if p == 0:
                    dve.wait_ge(offs_in, 32)
                for j in (2, 3):
                    for m in range(PT):
                        s = PT * p + m
                        h, r = hid[j][:, s, :], stat[:, RSTD + s:RSTD + s + 1]
                        if j == 2:
                            dve.wait_ge(gf_done, PT * (3 * p + j) + m + 1)
                            dve.tensor_scalar(h, h, r, None, ALU.mult).then_inc(fin_done, 1)
                        else:
                            dve.scalar_tensor_tensor(out=h, in0=h, scalar=r, in1=gfin[:, 3 * BLK:4 * BLK],
                                                     op0=ALU.mult, op1=ALU.mult).then_inc(fin_done, 1)

            for i, (_, k) in enumerate(LAST):
                if i + 2 < len(LAST):
                    last_lo(i + 2)
                if k % 2:
                    last_add(k // 2)
            for p in range(PASSES):
                if p:
                    for j in range(4):
                        last_add(4 * p + j)
                final_scale(p)


_NAMES = ["x", "norm1_g", "w_in", "gf_up", "gf_b", "gb_up", "gb_b", "gla_norm_g", "attn_norm_g", "w_out",
          "norm2_g", "w_gate", "w_up", "conv_w", "conv_b", "w_down", "final_norm_g"]


def kernel(**inputs):
    import concourse.bacc as bacc
    from concourse.bass_utils import run_bass_kernel_spmd

    nc = bacc.Bacc("TRN2", target_bir_lowering=False, num_devices=1)
    arrays = {f"in_{k}": np.ascontiguousarray(inputs[k]) for k in _NAMES}
    arrays.update({f"in_{k}": np.ascontiguousarray(v) for k, v in
                   zip(("tables", "toep", "rope", "masks"), constant_tables())})
    aps = [nc.dram_tensor(k, a.shape, mybir.dt.from_np(a.dtype), kind="ExternalInput").ap() for k, a in arrays.items()]
    out = nc.dram_tensor("out", inputs["x"].shape, F32, kind="ExternalOutput").ap()
    encoder_block(nc, *aps, out)
    r = run_bass_kernel_spmd(nc, [arrays], core_ids=[0])
    return r.results[0]["out"]
```
